# Optimizing a Trainium2 kernel written in Bass

```python
import math
import jax, jax.numpy as jnp
from jax import lax
import numpy as np

D_MODEL = 1024
BATCH = 1
SEQ = 2048
DEPTH = 1

POOL_WIDTH = D_MODEL // 4
POOL_GROUPS = 4
POOL_GDIM = POOL_WIDTH // POOL_GROUPS
POOL_WINDOWS = (2, 4, 8, 16)
HEAD_DIM = 128
ATTN_WIDTH = D_MODEL - POOL_WIDTH
N_HEADS = ATTN_WIDTH // HEAD_DIM
N_KV_HEADS = 2
KV_WIDTH = N_KV_HEADS * HEAD_DIM
IDX_HEADS = 8
IDX_DIM = 64
TOPK_MAX = 256
QBLK = 128
ROPE_THETA = 500000.0
ROPE_DIM = HEAD_DIM // 4
IDX_ROPE_DIM = IDX_DIM // 4
N_EXPERTS = 32
TOP_K = 4
D_FF = D_MODEL
SWIGLU_LIMIT = 7.0
SWIGLU_ALPHA = 1.702
ALPHA_RES = (2.0 * DEPTH) ** 0.25
BETA_INIT = (8.0 * DEPTH) ** -0.25
LN_EPS = 1e-5
NEG_INF = -1e30
OFF_POOL = 0
OFF_Q = OFF_POOL + POOL_WIDTH
OFF_K = OFF_Q + ATTN_WIDTH
OFF_V = OFF_K + KV_WIDTH
OFF_IQ = OFF_V + KV_WIDTH
OFF_IK = OFF_IQ + IDX_HEADS * IDX_DIM
OFF_IW = OFF_IK + IDX_DIM
IN_WIDTH = OFF_IW + IDX_HEADS

kernel_name = "hymba_pool_dsa_moe_deepnorm"

def layer_norm(x, g, b):
    xf = x.astype(jnp.float32)
    mu = jnp.mean(xf, axis=-1, keepdims=True)
    var = jnp.mean(jnp.square(xf - mu), axis=-1, keepdims=True)
    y = (xf - mu) * lax.rsqrt(var + LN_EPS) * g.astype(jnp.float32) + b.astype(jnp.float32)
    return y.astype(x.dtype)

def apply_rope(x, positions, rd):
    inv_freq = ROPE_THETA ** (-jnp.arange(0, rd, 2, dtype=jnp.float32) / rd)
    ang = positions.astype(jnp.float32)[..., None] * inv_freq
    cos = jnp.cos(ang)[:, :, None, :]
    sin = jnp.sin(ang)[:, :, None, :]
    xr = x[..., :rd].astype(jnp.float32)
    x1, x2 = xr[..., : rd // 2], xr[..., rd // 2:]
    rot = jnp.concatenate([x1 * cos - x2 * sin, x2 * cos + x1 * sin], axis=-1)
    return jnp.concatenate([rot.astype(x.dtype), x[..., rd:]], axis=-1)

def pool_mixer(u, w_pool, pool_scale):
    B, L, C = u.shape
    uf = u.astype(jnp.float32)
    cs = jnp.concatenate([jnp.zeros((B, 1, C), jnp.float32), jnp.cumsum(uf, axis=1)], axis=1)
    t = jnp.arange(L)
    diffs = []
    for gi, w in enumerate(POOL_WINDOWS):
        sl = slice(gi * POOL_GDIM, (gi + 1) * POOL_GDIM)
        c = cs[..., sl]
        lo = jnp.maximum(t + 1 - w, 0)
        win_sum = c[:, t + 1] - c[:, lo]
        cnt = jnp.minimum(t + 1, w).astype(jnp.float32)[None, :, None]
        diffs.append(win_sum / cnt - uf[..., sl])
    d = jnp.stack(diffs, axis=2)
    y = jnp.einsum('blgc,gcd->blgd', d, w_pool.astype(jnp.float32)).reshape(B, L, C)
    return (y * pool_scale.astype(jnp.float32)).astype(u.dtype)

def sparse_attention(q, k, v, iq, ik, iw):
    B, L = q.shape[:2]
    n_sel = min(TOPK_MAX, L // 4)
    nb = L // QBLK
    key_pos = jnp.arange(L)
    ikf = ik.astype(jnp.float32)
    w_scale = (IDX_HEADS ** -0.5) * (IDX_DIM ** -0.5)

    def to_blocks(a):
        return a.reshape((B, nb, QBLK) + a.shape[2:]).swapaxes(0, 1)

    def block(args):
        qb, iqb, iwb, q_pos = args
        s = jnp.einsum('bqhd,bsd->bqhs', iqb.astype(jnp.float32), ikf)
        idx_score = jnp.einsum('bqhs,bqh->bqs', jax.nn.relu(s), iwb.astype(jnp.float32) * w_scale)
        causal = key_pos[None, :] <= q_pos[:, None]
        idx_score = jnp.where(causal[None], idx_score, NEG_INF)
        _, sel = lax.top_k(idx_score, n_sel)
        k_sel = jax.vmap(lambda kb, ib: kb[ib])(k, sel)
        v_sel = jax.vmap(lambda vb, ib: vb[ib])(v, sel)
        qg = qb.reshape(B, QBLK, N_KV_HEADS, N_HEADS // N_KV_HEADS, HEAD_DIM).astype(jnp.float32)
        logits = jnp.einsum('bqgrd,bqkgd->bqgrk', qg, k_sel.astype(jnp.float32)) * (HEAD_DIM ** -0.5)
        valid = sel <= q_pos[None, :, None]
        logits = jnp.where(valid[:, :, None, None, :], logits, NEG_INF)
        p = jax.nn.softmax(logits, axis=-1)
        o = jnp.einsum('bqgrk,bqkgd->bqgrd', p, v_sel.astype(jnp.float32))
        return o.reshape(B, QBLK, ATTN_WIDTH).astype(q.dtype)

    out = lax.map(block, (to_blocks(q), to_blocks(iq), to_blocks(iw), key_pos.reshape(nb, QBLK)))
    return out.swapaxes(0, 1).reshape(B, L, ATTN_WIDTH)

def moe(h, w_router, b_router, w_gate_up, b_gate_up, w_down, b_down):
    B, L, D = h.shape
    xf = h.reshape(-1, D)
    logits = xf.astype(jnp.float32) @ w_router.astype(jnp.float32) + b_router.astype(jnp.float32)
    top_logit, top_e = lax.top_k(logits, TOP_K)
    gates = jax.nn.softmax(top_logit, axis=-1)
    flat_e = top_e.reshape(-1)
    order = jnp.argsort(flat_e)
    e_sorted = flat_e[order]
    tok = order // TOP_K
    g_sorted = gates.reshape(-1)[order]
    group_sizes = jnp.bincount(flat_e, length=N_EXPERTS).astype(jnp.int32)
    xs = xf[tok]
    hu = lax.ragged_dot(xs, w_gate_up, group_sizes) + b_gate_up[e_sorted]
    gate = jnp.minimum(hu[:, :D_FF], SWIGLU_LIMIT)
    up = jnp.clip(hu[:, D_FF:], -SWIGLU_LIMIT, SWIGLU_LIMIT)
    act = (up + 1.0) * gate * jax.nn.sigmoid(SWIGLU_ALPHA * gate)
    y = lax.ragged_dot(act, w_down, group_sizes) + b_down[e_sorted]
    y = y * g_sorted[:, None].astype(y.dtype)
    out = jnp.zeros_like(xf).at[tok].add(y)
    return out.reshape(B, L, D)

def setup_inputs(seed: int = 0) -> dict:
    key = jax.random.key(seed)
    ks = jax.random.split(key, 20)
    f32 = jnp.float32
    nrm = lambda k, shape: jax.random.normal(k, shape, f32)
    x = nrm(ks[0], (BATCH, SEQ, D_MODEL))
    offs = jax.random.randint(ks[1], (BATCH, 1), 0, 4096, dtype=jnp.int32)
    positions = (offs + jnp.arange(SEQ, dtype=jnp.int32)[None, :]).astype(jnp.int32)
    ln_in_g = 1.0 + 0.02 * nrm(ks[2], (D_MODEL,))
    ln_in_b = 0.02 * nrm(ks[3], (D_MODEL,))
    col_scale = jnp.concatenate([
        jnp.ones((OFF_V,), f32),
        jnp.full((KV_WIDTH,), BETA_INIT, f32),
        jnp.ones((IN_WIDTH - OFF_IQ,), f32)])
    w_in = nrm(ks[4], (DEPTH, D_MODEL, IN_WIDTH)) * (D_MODEL ** -0.5) * col_scale
    w_pool = nrm(ks[5], (DEPTH, POOL_GROUPS, POOL_GDIM, POOL_GDIM)) * (POOL_GDIM ** -0.5)
    pool_scale = 1.0 + 0.02 * nrm(ks[6], (DEPTH, POOL_WIDTH))
    w_out = nrm(ks[7], (DEPTH, D_MODEL, D_MODEL)) * (D_MODEL ** -0.5) * BETA_INIT
    ln1_g = 1.0 + 0.02 * nrm(ks[8], (DEPTH, D_MODEL))
    ln1_b = 0.02 * nrm(ks[9], (DEPTH, D_MODEL))
    w_router = nrm(ks[10], (DEPTH, D_MODEL, N_EXPERTS)) * (D_MODEL ** -0.5)
    b_router = 0.01 * nrm(ks[11], (DEPTH, N_EXPERTS))
    w_gate_up = nrm(ks[12], (DEPTH, N_EXPERTS, D_MODEL, 2 * D_FF)) * (D_MODEL ** -0.5) * BETA_INIT
    b_gate_up = 0.01 * nrm(ks[13], (DEPTH, N_EXPERTS, 2 * D_FF))
    w_down = nrm(ks[14], (DEPTH, N_EXPERTS, D_FF, D_MODEL)) * (D_FF ** -0.5) * BETA_INIT
    b_down = 0.01 * nrm(ks[15], (DEPTH, N_EXPERTS, D_MODEL))
    ln2_g = 1.0 + 0.02 * nrm(ks[16], (DEPTH, D_MODEL))
    ln2_b = 0.02 * nrm(ks[17], (DEPTH, D_MODEL))
    return {"x": x, "positions": positions, "ln_in_g": ln_in_g, "ln_in_b": ln_in_b,
            "w_in": w_in, "w_pool": w_pool, "pool_scale": pool_scale, "w_out": w_out,
            "ln1_g": ln1_g, "ln1_b": ln1_b, "w_router": w_router, "b_router": b_router,
            "w_gate_up": w_gate_up, "b_gate_up": b_gate_up, "w_down": w_down, "b_down": b_down,
            "ln2_g": ln2_g, "ln2_b": ln2_b}

def reference(x, positions, ln_in_g, ln_in_b, w_in, w_pool, pool_scale, w_out, ln1_g, ln1_b,
              w_router, b_router, w_gate_up, b_gate_up, w_down, b_down, ln2_g, ln2_b):
    B, L, _ = x.shape
    h = layer_norm(x, ln_in_g, ln_in_b)
    for l in range(DEPTH):
        proj = jnp.einsum('bld,de->ble', h, w_in[l])
        u = proj[..., OFF_POOL:OFF_Q]
        q = proj[..., OFF_Q:OFF_K].reshape(B, L, N_HEADS, HEAD_DIM)
        k = proj[..., OFF_K:OFF_V].reshape(B, L, N_KV_HEADS, HEAD_DIM)
        v = proj[..., OFF_V:OFF_IQ].reshape(B, L, N_KV_HEADS, HEAD_DIM)
        iq = proj[..., OFF_IQ:OFF_IK].reshape(B, L, IDX_HEADS, IDX_DIM)
        ik = proj[..., OFF_IK:OFF_IW].reshape(B, L, 1, IDX_DIM)
        iw = proj[..., OFF_IW:IN_WIDTH]
        q = apply_rope(q, positions, ROPE_DIM)
        k = apply_rope(k, positions, ROPE_DIM)
        iq = apply_rope(iq, positions, IDX_ROPE_DIM)
        ik = apply_rope(ik, positions, IDX_ROPE_DIM)[:, :, 0, :]
        pool_out = pool_mixer(u, w_pool[l], pool_scale[l])
        attn_out = sparse_attention(q, k, v, iq, ik, iw)
        mix = jnp.einsum('ble,ed->bld', jnp.concatenate([pool_out, attn_out], axis=-1), w_out[l])
        h = layer_norm(ALPHA_RES * h + mix, ln1_g[l], ln1_b[l])
        ffn = moe(h, w_router[l], b_router[l], w_gate_up[l], b_gate_up[l], w_down[l], b_down[l])
        h = layer_norm(ALPHA_RES * h + ffn, ln2_g[l], ln2_b[l])
    return h


_drawn_inputs = setup_inputs


def setup_inputs(seed=0):
    import zlib

    import numpy as np

    out = dict(_drawn_inputs(seed))
    spreads = {}
    factors = {'pool_scale': 21.848,
     'b_router': 6.923,
     'b_gate_up': 26.095,
     'b_down': 8.0,
     'ln2_g': 8.179,
     'ln2_b': 8.214,
     'ln_in_b': 4.45}
    for name, (base, spread) in spreads.items():
        noise = np.random.default_rng([zlib.crc32(name.encode()), seed]).standard_normal(out[name].shape)
        drawn = base * np.exp(spread * noise) if base else spread * noise
        out[name] = __import__('jax').numpy.asarray(drawn.astype(out[name].dtype))
    for name, factor in factors.items():
        out[name] = (out[name] * factor).astype(out[name].dtype)
    return out
```

```python
from contextlib import ExitStack

import numpy as np

import concourse.bass as bass
from concourse import mybir

F32 = mybir.dt.float32
F32R = mybir.dt.float32r
I32 = mybir.dt.int32
U32 = mybir.dt.uint32
BF16 = mybir.dt.bfloat16
ALU = mybir.AluOpType
ACT = mybir.ActivationFunctionType
AX = mybir.AxisListType.X

P = 128
SEQ = 2048
D = 1024
TILES = SEQ // P
KD = D // P
POOL_W, POOL_GROUPS = D // 4, 4
POOL_G = POOL_W // POOL_GROUPS
WINDOWS = (2, 4, 8, 16)
HEAD = 128
HEADS = (D - POOL_W) // HEAD
KV = 2
REP = HEADS // KV
IDX_H, IDX_D = 8, 64
TOPK = min(256, SEQ // 4)
THETA = 500000.0
ROPE_D, IDX_ROPE_D = HEAD // 4, IDX_D // 4
NF, NFI = ROPE_D // 2, IDX_ROPE_D // 2
EXPERTS, TOP_E, FF = 32, 4, D
LIMIT, SWI_ALPHA = 7.0, 1.702
ALPHA_RES = 2.0 ** 0.25
EPS = 1e-5
NEG = -1e30
OFF_Q = POOL_W
OFF_K = OFF_Q + HEADS * HEAD
OFF_V = OFF_K + KV * HEAD
OFF_IQ = OFF_V + KV * HEAD
OFF_IK = OFF_IQ + IDX_H * IDX_D
OFF_IW = OFF_IK + IDX_D
IN_W = OFF_IW + IDX_H
BANK = 512
NQI = HEADS + IDX_H * IDX_D // P
ROT = (HEADS + KV) * HEAD
ROWS = 3 * P
WIDTHS = (2 * P, 2 * P + 64, ROWS)
MAX_VISITS = EXPERTS + SEQ * TOP_E // ROWS
META = MAX_VISITS + 1
TAIL = 8 * P
CHUNK = 4096


def wait(eng, sem, value):
    if not isinstance(value, int) or value > 0:
        eng.wait_ge(sem, value)


def project_stage(nc, A, S, D_):
    with ExitStack() as ctx:
        def sb(name, shape, dt=F32):
            return ctx.enter_context(nc.sbuf_tensor(name, shape, dt))

        def sem(name):
            return ctx.enter_context(nc.semaphore(name))

        w_in = sb("w_in_sb", [P, KD, IN_W])
        x_in = sb("x_in", [P, 2, D])
        h = sb("h_norm", [P, 2, D])
        hT = sb("hT", [P, 2, KD, P])
        rot = sb("rot", [P, 2, ROT + (IDX_H + 2) * IDX_D])
        stage = sb("qi_stage", [P, 2, NQI, P])
        gain = sb("gain_in", [P, D])
        bias = sb("bias_in", [P, D])
        pos_i = sb("pos_i", [P, TILES], I32)
        pos_f = sb("pos_f", [P, TILES])
        inv_f = sb("inv_f", [P, NF + NFI])
        ang = sb("ang", [P, TILES, NF + NFI])
        turns = sb("turns", [P, TILES, NF + NFI])
        turns_i = sb("turns_i", [P, TILES, NF + NFI], I32)
        cos = sb("cos", [P, TILES, NF + NFI])
        sin = sb("sin", [P, TILES, NF + NFI])
        prod = sb("rope_prod", [P, 4, (HEADS + KV) * NF + (IDX_H + 1) * NFI])
        zeros = sb("zeros", [P, D])
        stats = sb("stats1", [P, 12])
        mean_var = sb("mean_var1", [P, 2])
        var_eps = sb("var_eps1", [P, 1])
        minus_half = sb("minus_half1", [P, 1])
        rstd = sb("rstd1", [P, 1])
        acc = ctx.enter_context(nc.psum_tensor("proj_acc", [P, 5, BANK], F32))
        tr = ctx.enter_context(nc.psum_tensor("proj_tr", [P, 3, 4, P], F32))

        s_clear = sem("p_clear")
        s_const = sem("p_const")
        s_win = sem("p_win")
        s_x = [sem("p_x0"), sem("p_x1")]
        s_var = sem("p_var")
        s_rstd = sem("p_rstd")
        s_half = sem("p_half")
        s_h = sem("p_h")
        s_hst = [sem("p_hst0"), sem("p_hst1")]
        s_th = sem("p_th")
        s_hT = sem("p_hT")
        s_tq = sem("p_tq")
        s_qi = sem("p_qi")
        s_pj = sem("p_pj")
        s_pjf = sem("p_pjf")
        s_trig = sem("p_trig")
        s_rot = sem("p_rot")
        s_qst = [sem("p_qst0"), sem("p_qst1")]

        CHUNKS = [(n * BANK, min(BANK, IN_W - n * BANK)) for n in range(5)]
        SHARE = (MAX_VISITS - EXPERTS) * ROWS // TILES
        SHARE_N = next(n for n in range(1, SHARE + 1) if SHARE % n == 0 and SHARE // n <= P)
        assert SHARE * TILES == (MAX_VISITS - EXPERTS) * ROWS

        def pairs(eng, body):
            for t in range(3):
                body(t, t % 2, t // 2)
            with eng.Fori(1, TILES // 2 - 1) as i:
                body(2 * i + 1, 1, i)
                body(2 * i + 2, 0, i + 1)
            body(TILES - 1, 1, TILES // 2 - 1)

        with nc.Block() as block:
            @block.sync
            def _(sp):
                sp.dma_start(gain[:], A["ln_in_g"].partition_broadcast(P)).then_inc(s_const, 16)
                sp.dma_start(bias[:], A["ln_in_b"].partition_broadcast(P)).then_inc(s_const, 16)
                sp.dma_start(inv_f[:], A["inv_freq"].partition_broadcast(P)).then_inc(s_const, 16)
                sp.dma_start(pos_i[:], A["positions"].rearrange("b (t p) -> p (b t)", p=P),
                             allow_slow_non_contiguous=True).then_inc(s_const, 16)

                def load_x(t, slot):
                    sp.dma_start(x_in[:, slot], D_["x"][bass.ds(t * P, P), :]).then_inc(s_x[slot], 16)

                load_x(0, 0)
                sp.wait_ge(s_half, 3)
                sp.dma_start(w_in[:], A["w_in"].rearrange("l (k p) n -> p (l k) n", p=P)).then_inc(s_win, 16)

                def body(t, slot, half):
                    if not (isinstance(t, int) and t == TILES - 1):
                        wait(sp, s_h, t)
                        load_x(t + 1, 1 - slot)
                    sp.wait_ge(s_h, t + 1)
                    sp.dma_start(D_["h"][bass.ds(t * P, P), :], h[:, slot]).then_inc(s_hst[slot], 16)
                    sp.dma_start(D_["y"][bass.ds(EXPERTS * ROWS + t * SHARE, SHARE), :].rearrange(
                        "(p n) d -> p n d", n=SHARE_N), zeros[0:SHARE // SHARE_N].unsqueeze(1).broadcast_to(
                        [SHARE // SHARE_N, SHARE_N, D])).then_inc(s_clear, 16)

                pairs(sp, body)
                sp.wait_ge(s_clear, 16 * TILES)
                sp.wait_ge(s_hst[0], 8 * TILES)
                sp.wait_ge(s_hst[1], 8 * TILES)

            @block.gpsimd
            def _(pool):
                nc.gpsimd.memset(S["ident"][:], 0.0).then_inc(s_half, 1)
                nc.gpsimd.memset(minus_half[:], -0.5).then_inc(s_half, 1)
                nc.gpsimd.memset(zeros[:], 0.0).then_inc(s_half, 1)
                pool.wait_ge(s_half, 3)
                nc.gpsimd.affine_select(out=S["ident"][:], in_=S["ident"][:], compare_op=ALU.not_equal,
                                        fill=1.0, base=0, pattern=[[-1, P]], channel_multiplier=1
                                        ).then_inc(s_half, 1)
                with pool.Fori(0, TILES) as t:
                    pool.wait_ge(s_var, t + 1)
                    nc.gpsimd.tensor_tensor(rstd[:], var_eps[:], minus_half[:], ALU.pow).then_inc(s_rstd, 1)

            @block.vector
            def _(dve):
                dve.wait_ge(s_const, 64)
                nc.vector.tensor_copy(pos_f[:], pos_i[:])
                dve.drain()
                shape = [P, TILES, NF + NFI]
                nc.vector.tensor_tensor(ang[:], pos_f[:].unsqueeze(2).broadcast_to(shape),
                                        inv_f[:].unsqueeze(1).broadcast_to(shape), ALU.mult)
                dve.drain()
                for out, quarter in ((sin, 0.0), (cos, 0.25)):
                    nc.vector.tensor_scalar(turns[:], ang[:], 1.0 / (2.0 * np.pi), quarter, ALU.mult, ALU.add)
                    dve.drain()
                    nc.vector.tensor_copy(turns_i[:], turns[:])
                    dve.drain()
                    nc.vector.tensor_copy(turns[:], turns_i[:])
                    dve.drain()
                    two_pi, src = 2.0 * np.pi, ang
                    for part in (6.28125, float(np.float32(two_pi - 6.28125) // 2 ** -19 * 2 ** -19), None):
                        part = two_pi if part is None else part
                        two_pi -= part
                        nc.vector.scalar_tensor_tensor(out[:], turns[:], -part, src[:], ALU.mult, ALU.add)
                        dve.drain()
                        src = out
                    nc.vector.tensor_scalar(out[:], out[:], quarter * 2.0 * np.pi, float(np.float32(3.1415925)),
                                            ALU.add, ALU.min)
                    dve.drain()
                    nc.vector.tensor_scalar(out[:], out[:], -float(np.float32(3.1415925)), None,
                                            ALU.max).then_inc(s_trig, 1)

                def norm(t, slot, half):
                    dve.wait_ge(s_x[slot], 16 * (half + 1))
                    nc.vector.bn_stats(stats[:, 0:6], x_in[:, slot, 0:512])
                    nc.vector.bn_stats(stats[:, 6:12], x_in[:, slot, 512:1024])
                    dve.drain()
                    nc.vector.bn_aggr(mean_var[:], stats[:])
                    dve.drain()
                    nc.vector.tensor_scalar(var_eps[:], mean_var[:, 1:2], EPS, None, ALU.add).then_inc(s_var, 1)
                    dve.wait_ge(s_rstd, t + 1)
                    wait(dve, s_th, 2 * t - 2)
                    if not isinstance(t, int) or t >= 2:
                        dve.wait_ge(s_hst[slot], 16 * half)
                    nc.vector.tensor_scalar(h[:, slot], x_in[:, slot], mean_var[:, 0:1], rstd[:],
                                            ALU.subtract, ALU.mult)
                    dve.drain()
                    nc.vector.tensor_tensor(h[:, slot], h[:, slot], gain[:], ALU.mult)
                    dve.drain()
                    nc.vector.tensor_tensor(h[:, slot], h[:, slot], bias[:], ALU.add).then_inc(s_h, 1)

                def rotate(t, slot):
                    at = 0
                    halves = []
                    for base, heads, width, nf, f0 in ((0, HEADS + KV, HEAD, NF, 0),
                                                       (ROT, IDX_H + 1, IDX_D, NFI, NF)):
                        xs = rot[:, slot, base:base + heads * width].rearrange("p (h d) -> p h d", d=width)
                        shape = [P, heads, nf]
                        c = cos[:, t, f0:f0 + nf].unsqueeze(1).broadcast_to(shape)
                        s = sin[:, t, f0:f0 + nf].unsqueeze(1).broadcast_to(shape)
                        x1, x2 = xs[:, :, 0:nf], xs[:, :, nf:2 * nf]
                        o = [prod[:, j, at:at + heads * nf].rearrange("p (h d) -> p h d", d=nf) for j in range(4)]
                        at += heads * nf
                        for out, a, b in ((o[0], x1, c), (o[1], x2, s), (o[2], x2, c), (o[3], x1, s)):
                            nc.vector.tensor_tensor(out, a, b, ALU.mult)
                        halves.append((x1, x2, o))
                    dve.drain()
                    for x1, x2, o in halves:
                        nc.vector.tensor_tensor(x1, o[0], o[1], ALU.subtract)
                        nc.vector.tensor_tensor(x2, o[2], o[3], ALU.add)
                    dve.drain()
                    ik = ROT + IDX_H * IDX_D
                    nc.vector.tensor_copy(rot[:, slot, ik + IDX_D:ik + 2 * IDX_D],
                                          rot[:, slot, ik:ik + IDX_D]).then_inc(s_rot, 1)

                norm(0, 0, 0)
                dve.wait_ge(s_trig, 4)

                def body(t, slot, half):
                    if not (isinstance(t, int) and t == TILES - 1):
                        norm(t + 1, 1 - slot, half if slot == 0 else half + 1)
                    dve.wait_ge(s_pjf, 5 * t + 5)
                    rotate(t, slot)

                pairs(dve, body)

            @block.tensor
            def _(pe):
                def transpose_h(t, slot):
                    pe.wait_ge(s_h, t + 1)
                    for g in range(2):
                        wait(pe, s_hT, 2 * t + g)
                        for j in range(4):
                            mm = nc.tensor.transpose(tr[:, 0, j], h[:, slot, (4 * g + j) * P:(4 * g + j + 1) * P],
                                                     S["ident"][:])
                        mm.then_inc(s_th, 1)

                def transpose_q(t, slot):
                    pe.wait_ge(s_rot, t + 1)
                    for g in range(4):
                        wait(pe, s_qi, 4 * t + g - 1)
                        for j in range(4 if g < 3 else 1):
                            mm = nc.tensor.transpose(tr[:, 1 + g % 2, j],
                                                     rot[:, slot, (4 * g + j) * P:(4 * g + j + 1) * P], S["ident"][:])
                        mm.then_inc(s_tq, 1)

                def project(t, slot):
                    pe.wait_ge(s_hT, 2 * t + 2)
                    for n, (c0, width) in enumerate(CHUNKS):
                        wait(pe, s_pjf, 5 * (t - 1) + n + 1)
                        for k in range(KD):
                            mm = nc.tensor.matmul(acc[:, n, 0:width], hT[:, slot, k], w_in[:, k, c0:c0 + width],
                                                  start=(k == 0), stop=(k == KD - 1))
                        mm.then_inc(s_pj, 1)

                pe.wait_ge(s_half, 4)
                transpose_h(0, 0)
                pe.wait_ge(s_win, 16)

                def body(t, slot, half):
                    project(t, slot)
                    if not (isinstance(t, int) and t == TILES - 1):
                        transpose_h(t + 1, 1 - slot)
                    if not isinstance(t, int) or t:
                        transpose_q(t - 1, 1 - slot)

                pairs(pe, body)
                transpose_q(TILES - 1, 1)

            @block.scalar
            def _(act):
                for j, out in enumerate((sin, cos)):
                    act.wait_ge(s_trig, j + 1 if j == 0 else 2)
                    if j == 0:
                        act.wait_ge(s_trig, 2)
                    nc.scalar.activation(out[:], out[:], ACT.Sin).then_inc(s_trig, 1)

                def out_of_h(t, slot):
                    wait(act, s_pj, 5 * (t - 1))
                    for g in range(2):
                        act.wait_ge(s_th, 2 * t + g + 1)
                        nc.scalar.activation(hT[:, slot, 4 * g:4 * g + 4], tr[:, 0], ACT.Copy).then_inc(s_hT, 1)

                def out_of_q(t, slot, half):
                    if not isinstance(t, int) or t >= 2:
                        act.wait_ge(s_qst[slot], 16 * half)
                    act.wait_ge(s_tq, 4 * t + 1)
                    nc.scalar.activation(stage[:, slot, 0:4], tr[:, 1], ACT.Copy).then_inc(s_qi, 1)
                    act.wait_ge(s_tq, 4 * t + 2)
                    nc.scalar.activation(stage[:, slot, 4:6], tr[:, 2, 0:2], ACT.Copy)
                    nc.scalar.activation(S["kT"][:, :, bass.ds(t * P, P)], tr[:, 2, 2:4], ACT.Copy).then_inc(s_qi, 1)
                    act.wait_ge(s_tq, 4 * t + 3)
                    nc.scalar.activation(stage[:, slot, 6:10], tr[:, 1], ACT.Copy).then_inc(s_qi, 1)
                    act.wait_ge(s_tq, 4 * t + 4)
                    nc.scalar.activation(S["ikT"][:, bass.ds(t * P, P)], tr[:, 2, 0], ACT.Copy).then_inc(s_qi, 1)
                    act.wait_ge(s_qi, 4 * t + 4)
                    nc.scalar.dma_start(D_["qi"][bass.ds(t * P, P), :], stage[:, slot].rearrange("p c n -> p (c n)")
                                        ).then_inc(s_qst[slot], 16)

                def out_of_projection(t, slot):
                    wait(act, s_tq, 4 * (t - 1))
                    dst = [[(S["u"][:, t], 0, 256), (rot[:, slot, 0:256], 256, 512)],
                           [(rot[:, slot, 256:768], 0, 512)],
                           [(rot[:, slot, 768:1024], 0, 256), (S["v"][:, t], 256, 512)],
                           [(rot[:, slot, ROT:ROT + 512], 0, 512)],
                           [(rot[:, slot, ROT + 512:ROT + 576], 0, 64)]]
                    for n in range(5):
                        act.wait_ge(s_pj, 5 * t + n + 1)
                        for out, a, b in dst[n]:
                            op = nc.scalar.activation(out, acc[:, n, a:b], ACT.Copy)
                        if n == 4:
                            op = nc.scalar.activation(S["iw"][:, t], acc[:, n, 64:72], ACT.Copy,
                                                      scale=float(np.float32((IDX_H ** -0.5) * (IDX_D ** -0.5))))
                        op.then_inc(s_pjf, 1)

                out_of_h(0, 0)

                def body(t, slot, half):
                    out_of_projection(t, slot)
                    if not (isinstance(t, int) and t == TILES - 1):
                        out_of_h(t + 1, 1 - slot)
                    if not isinstance(t, int) or t:
                        out_of_q(t - 1, 1 - slot, half if slot == 1 else half - 1)

                pairs(act, body)
                out_of_q(TILES - 1, 1, TILES // 2 - 1)
                act.wait_ge(s_qst[0], 8 * TILES)
                act.wait_ge(s_qst[1], 8 * TILES)


def attend_stage(nc, A, S, D_):
    SCALE = HEAD ** -0.5
    CLEARS = 16 * 2
    CONSTS = 16 * 13
    keys = [P * (b + 1) for b in range(TILES)]
    chunks = [-(-k // BANK) if k > TOPK else 0 for k in keys]
    chunk0 = [sum(chunks[:b]) for b in range(TILES + 1)]
    pv0 = [sum(2 * (j + 1) for j in range(b)) for b in range(TILES + 1)]

    BITS, SELECT = 32, 5

    def parts(b):
        s = b - 1
        width = [min(BANK, max(0, (keys[s + 2] if s + 2 < TILES else 0) - c * BANK)) for c in range(4)]
        group = 2 * REP * P
        work = [(KD + 1) * D, 2 * IDX_H * width[0], 2 * IDX_H * width[1], (s + 1) * group,
                2 * IDX_H * width[2] + D, 2 * IDX_H * width[3] + D + (s + 1) * group]
        work = [w + keys[s] for w in work]
        return [min(BITS, round((BITS + SELECT) * sum(work[:i + 1]) / sum(work))) if i < HEADS - 1 else BITS
                for i in range(HEADS)]

    def walk(do):
        def piece(name, b, *at):
            if 0 <= b < TILES and name in do:
                do[name](b, *at)

        def fill(b, i, *pieces):
            head = (b, i) if b < TILES else None
            for name, of, *at in pieces:
                if 0 <= of < TILES and (name != "score" or at[0] < chunks[of]):
                    piece(name, of, *at, head)
                    head = None
            if head:
                piece("exp", b, i)

        def search(b, i):
            if 2 <= b:
                piece("search", b, i)

        for b in range(TILES + 2):
            piece("logits", b, 0)
            piece("choose", b - 2)
            search(b + 1, 0)
            fill(b, 0, ("project", b - 1))
            piece("logits", b, 1)
            search(b + 1, 1)
            fill(b, 1, ("score", b + 2, 0))
            piece("rank", b - 2)
            piece("logits", b, 2)
            piece("statistics", b - 1)
            search(b + 1, 2)
            fill(b, 2, ("score", b + 2, 1))
            piece("norm", b - 1)
            piece("logits", b, 3)
            piece("inverse", b, 0)
            piece("weigh", b - 2)
            search(b + 1, 3)
            fill(b, 3, ("values", b, 0))
            piece("logits", b, 4)
            search(b + 1, 4)
            fill(b, 4, ("score", b + 2, 2))
            piece("differ", b)
            piece("transpose", b - 1)
            piece("pool", b)
            piece("logits", b, 5)
            search(b + 1, 5)
            fill(b, 5, ("score", b + 2, 3))
            piece("prepare", b + 3)
            piece("route", b - 1)
            piece("scatter", b - 2)
            piece("inverse", b, 1)
            if 2 <= b + 1:
                piece("select", b + 1)
            piece("values", b, 1, None)

    with ExitStack() as ctx:
        def sb(name, shape, dt=F32):
            return ctx.enter_context(nc.sbuf_tensor(name, shape, dt))

        def sem(name):
            return ctx.enter_context(nc.semaphore(name))

        w_out = sb("w_out_sb", [P, KD, D])
        w_router = sb("w_router_sb", [P, KD, EXPERTS])
        b_router = sb("b_router_sb", [P, EXPERTS])
        gain = sb("gain_1", [P, D])
        bias = sb("bias_1", [P, D])
        band = sb("band_sb", [P, 3, POOL_GROUPS, P])
        w_pool = sb("w_pool_sb", [P, 2, P])
        pool_scale = sb("pool_scale_sb", [P, 2])
        q = sb("q_blk", [P, 2, HEADS, P])
        iq = sb("iq_blk", [P, 2, NQI - HEADS, P])
        h = sb("h_blk", [P, D])
        scores = [sb("scores_even", [P, SEQ - P]), sb("scores_odd", [P, SEQ])]
        mask = sb("mask", [P, 2, SEQ], BF16)
        relu = sb("relu", [P, 2, BANK])
        w_diag = sb("w_diag", [P, IDX_H, P])
        probs = sb("probs", [P, 4, SEQ])
        probsT = sb("probsT", [P, 2, REP, P])
        r_diag = sb("r_diag", [P, REP, P])
        r_all = sb("r_all", [P, REP, P])
        oT = sb("oT", [P, REP, P])
        diffT = oT[:, 0:2]
        mixT = sb("mixT", [P, KD, P])
        res = sb("res", [P, D])
        h1 = res
        h1T = h[:].rearrange("p (k n) -> p k n", n=P)
        ident_bf = sb("ident_bf", [P, P], BF16)
        alpha_ident = sb("alpha_ident", [P, P])
        ones = sb("ones", [P, P])
        before = sb("before", [P, P])
        expert_no = sb("expert_no", [P, EXPERTS])
        small = sb("small", [P, 66])
        n_max, sums, inv_sum = small[:, 0:6], small[:, 8:14], small[:, 16:22]
        row_max = small[:, 24:25]
        stats, mean_var = small[:, 26:38], small[:, 38:40]
        var_eps, minus_half, rstd, shift = (small[:, j:j + 1] for j in (40, 41, 42, 43))
        best, n_best, e_sum, e_inv = small[:, 44:52], small[:, 52:53], small[:, 53:54], small[:, 54:55]
        bit_value = sb("bit_value_sb", [P, 32])
        bit_next = sb("bit_next_sb", [P, 32], I32)
        limit, n_reach, turn = small[:, 55:56], small[:, 56:57], small[:, 57:58].bitcast(I32)
        at_f = small[:, 58:62]
        at_i = sb("at_i", [P, TOP_E], I32)
        token = sb("token", [P, TILES], I32)
        e_gate = small[:, 62:66]
        best_at = sb("best_at", [P, 8], U32)
        best_no = sb("best_no", [P, 8])
        r_logits = sb("r_logits", [P, EXPERTS])
        pick_at = sb("pick_at", [P, TOP_E * EXPERTS])
        chosen = sb("chosen", [P, EXPERTS])
        so_far = S["so_far"]

        qk = ctx.enter_context(nc.psum_tensor("qk", [P, SEQ], F32))
        pair = ctx.enter_context(nc.psum_tensor("pair", [P, 2, BANK], F32))
        acc = ctx.enter_context(nc.psum_tensor("acc", [P, BANK], F32))
        o_acc = ctx.enter_context(nc.psum_tensor("o_acc", [P, REP, P], F32))

        s_const = sem("a_const")
        s_made = sem("a_made")
        s_q = [sem("a_q0"), sem("a_q1")]
        s_iq = [sem("a_iq0"), sem("a_iq1")]
        s_hl = sem("a_h")
        s_wd = sem("a_wd")
        s_idx = sem("a_idx")
        s_relu = sem("a_relu")
        s_wsum = sem("a_wsum")
        s_sc = sem("a_sc")
        s_causal = sem("a_causal")
        s_mask = sem("a_mask")
        s_qk = sem("a_qk")
        s_max = sem("a_max")
        s_exp = sem("a_exp")
        s_inv = sem("a_inv")
        s_rd = sem("a_rd")
        s_pt = sem("a_pt")
        s_pts = sem("a_pts")
        s_pv = sem("a_pv")
        s_ra = sem("a_ra")
        s_ov = sem("a_ov")
        s_mix = sem("a_mix")
        s_diff = sem("a_diff")
        s_diffs = sem("a_diffs")
        s_pool = sem("a_pool")
        s_pools = sem("a_pools")
        s_out = sem("a_out")
        s_res = sem("a_res")
        s_var = sem("a_var")
        s_rstd = sem("a_rstd")
        s_norm = sem("a_norm")
        s_h1 = sem("a_h1")
        s_h1st = sem("a_h1st")
        s_ht = sem("a_ht")
        s_hts = sem("a_hts")
        s_rl = sem("a_rl")
        s_best = sem("a_best")
        s_eg = sem("a_eg")
        s_gate = sem("a_gate")
        s_ch = sem("a_ch")
        s_rk = sem("a_rk")
        s_rks = sem("a_rks")
        s_cum = sem("a_cum")
        s_at = sem("a_at")
        s_clear = sem("a_clear")
        s_list = sem("a_list")

        with nc.Block() as block:
            @block.sync
            def _(sp):
                def load_iq(b):
                    if b >= 2 + 2:
                        sp.wait_ge(s_idx, IDX_H * chunk0[b - 1])
                    sp.dma_start(iq[:, b % 2], D_["qi"][b * P:(b + 1) * P, HEADS * P:].rearrange(
                        "p (c n) -> p c n", n=P)).then_inc(s_iq[b % 2], 16)

                def load_q(b):
                    wait(sp, s_qk, HEADS * (b - 1))
                    sp.dma_start(q[:, b % 2], D_["qi"][b * P:(b + 1) * P, 0:HEADS * P].rearrange(
                        "p (c n) -> p c n", n=P)).then_inc(s_q[b % 2], 16)

                load_q(0)
                sp.dma_start(pool_scale[:], A["pool_scale"].rearrange("l (c p) -> p (l c)", p=P),
                             allow_slow_non_contiguous=True).then_inc(s_const, 16)
                sp.dma_start(band[:], A["band"]).then_inc(s_const, 16)
                sp.wait_ge(s_made, 2)
                sp.dma_start(D_["lists"][0:EXPERTS * SEQ, :].rearrange("(p n) o -> p (n o)", p=P),
                             res[:, 0:EXPERTS * SEQ // P].bitcast(I32)).then_inc(s_clear, 16)
                sp.dma_start(D_["lists"][EXPERTS * SEQ:, :].rearrange("(p n) o -> p (n o)", p=P),
                             res[:, 0:TAIL // P].bitcast(I32)).then_inc(s_clear, 16)
                sp.wait_ge(s_made, 1)
                for g in range(POOL_GROUPS):
                    at = (g % 2) * POOL_G
                    sp.dma_start(w_pool[at:at + POOL_G, g // 2, at:at + POOL_G], A["w_pool"][0, g]
                                 ).then_inc(s_const, 16)
                load_q(1)
                load_iq(2)
                load_iq(3)
                for out, name in ((gain, "ln1_g"), (bias, "ln1_b"), (b_router, "b_router"),
                                  (bit_value, "bit_value"), (bit_next, "bit_next")):
                    sp.dma_start(out[:], A[name][0].partition_broadcast(P)).then_inc(s_const, 16)
                sp.dma_start(w_router[:], A["w_router"][0].rearrange("(k p) n -> p k n", p=P)).then_inc(s_const, 16)
                sp.dma_start(w_out[:], A["w_out"][0].rearrange("(k p) n -> p k n", p=P)).then_inc(s_const, 16)

                def fetch(b):
                    wait(sp, s_rl, b)
                    sp.dma_start(h[:], D_["h"][b * P:(b + 1) * P, :]).then_inc(s_hl, 16)

                def logits(b, i):
                    if i == 0:
                        if b + 3 < TILES and b >= 1:
                            load_iq(b + 3)
                        if b >= 1 and b + 1 < TILES:
                            load_q(b + 1)

                def store(b):
                    sp.wait_ge(s_h1, b + 1)
                    sp.dma_start(D_["h1"][b * P:(b + 1) * P, :], h1[:]).then_inc(s_h1st, 16)

                fetch(0)
                walk({"logits": logits, "norm": store, "route": lambda b: fetch(b + 1) if b + 1 < TILES else None})
                sp.wait_ge(s_h1st, 16 * TILES)

            @block.gpsimd
            def _(pool):
                nc.gpsimd.memset(w_pool[:], 0.0).then_inc(s_made, 1)
                nc.gpsimd.memset(ones[:], 1.0)
                nc.gpsimd.memset(minus_half, -0.5)
                nc.gpsimd.memset(res[:], 0.0)
                nc.gpsimd.memset(so_far[:], 0.0)
                nc.gpsimd.memset(before[:], 1.0)
                nc.gpsimd.memset(mask[:, :, 0:TOPK], 0.0)
                nc.gpsimd.iota(expert_no[:], pattern=[[1, EXPERTS]], base=0, channel_multiplier=0,
                               allow_small_or_imprecise_dtypes=True)
                nc.gpsimd.iota(token[:], pattern=[[P, TILES]], base=0, channel_multiplier=1)
                nc.gpsimd.tensor_copy(ident_bf[:], S["ident"][:])
                nc.gpsimd.tensor_scalar(alpha_ident[:], S["ident"][:], ALPHA_RES, 1.0, ALU.mult, ALU.mult
                                        ).then_inc(s_made, 1)
                pool.drain()
                pool.wait_ge(s_made, 2)
                nc.gpsimd.affine_select(out=before[:], in_=before[:], compare_op=ALU.is_gt, fill=0.0,
                                        base=0, pattern=[[1, P]], channel_multiplier=-1)
                for b in range(2):
                    nc.gpsimd.affine_select(out=mask[:, b, 0:keys[b]], in_=mask[:, b, 0:keys[b]],
                                            compare_op=ALU.is_ge, fill=NEG, base=b * P,
                                            pattern=[[-1, keys[b]]], channel_multiplier=1).then_inc(s_made, 1)

                def prepare(b):
                    wait(pool, s_wsum, IDX_H * chunk0[b])
                    for i in range(IDX_H):
                        op = nc.gpsimd.tensor_scalar(w_diag[:, i], S["ident"][:], S["iw"][:, b, i:i + 1], 1.0,
                                                     ALU.mult, ALU.mult)
                    op.then_inc(s_wd, 1)

                def score(b, c, head):
                    if c == chunks[b] - 1:
                        pool.wait_ge(s_sc, chunk0[b + 1])
                        tail = scores[b % 2][:, b * P:(b + 1) * P]
                        nc.gpsimd.affine_select(out=tail, in_=tail, compare_op=ALU.is_ge, fill=NEG, base=0,
                                                pattern=[[-1, P]], channel_multiplier=1).then_inc(s_causal, 1)

                def values(b, g, head):
                    n = KV * b + g
                    pool.wait_ge(s_inv, n + 1)
                    wait(pool, s_ra, n)
                    for j in range(REP):
                        op = nc.gpsimd.tensor_scalar(r_diag[:, j], S["ident"][:],
                                                     inv_sum[:, g * REP + j:g * REP + j + 1], 1.0, ALU.mult, ALU.mult)
                    op.then_inc(s_rd, 1)
                    pool.wait_ge(s_ov, 2 * n + 2)
                    wait(pool, s_out, b)
                    nc.gpsimd.tensor_tensor(mixT[:, 2 + g * REP:2 + (g + 1) * REP], oT[:], r_all[:], ALU.mult
                                            ).then_inc(s_mix, 1)

                def norm(b):
                    pool.wait_ge(s_var, b + 1)
                    nc.gpsimd.tensor_tensor(rstd, var_eps, minus_half, ALU.pow)
                    pool.drain()
                    nc.gpsimd.tensor_tensor(shift, mean_var[:, 0:1], rstd, ALU.mult)
                    pool.drain()
                    nc.gpsimd.tensor_scalar(shift, shift, -1.0, 1.0, ALU.mult, ALU.mult).then_inc(s_rstd, 1)
                    pool.wait_ge(s_norm, b + 1)
                    nc.gpsimd.tensor_tensor(h1[:], h1[:], gain[:], ALU.mult)
                    pool.drain()
                    nc.gpsimd.tensor_tensor(h1[:], h1[:], bias[:], ALU.add).then_inc(s_h1, 1)

                def scatter(b):
                    pool.wait_ge(s_at, b + 1)
                    for k in range(TOP_E):
                        nc.gpsimd.indirect_dma_start(
                            D_["lists"], bass.IndirectOffsetOnAxis(ap=at_i[:, k:k + 1], axis=0),
                            token[:, b:b + 1], None).then_inc(s_list, 16)
                    pool.wait_ge(s_list, 64 * (b + 1))

                def rank(b):
                    pool.wait_ge(s_rk, b + 1)
                    nc.gpsimd.tensor_tensor(so_far[:], so_far[:], chosen[:], ALU.add).then_inc(s_cum, 1)

                prepare(2)
                pool.wait_ge(s_const, CONSTS)

                pool.wait_ge(s_clear, CLEARS)
                walk({"prepare": prepare, "score": score, "values": values, "norm": norm, "rank": rank,
                      "scatter": scatter})

            @block.vector
            def _(dve):
                def search(b, first, last):
                    s, reach = scores[b % 2][:, 0:keys[b]], mask[:, b % 2, 0:keys[b]]
                    if first == 0:
                        nc.vector.memset(limit, 0.0)
                        dve.drain()
                    for i in range(first, last):
                        nc.vector.tensor_scalar(reach, s, limit, 0.0, ALU.is_ge, ALU.add, accum_out=n_reach)
                        dve.drain()
                        nc.vector.scalar_tensor_tensor(turn, n_reach, float(TOPK), bit_value[:, i:i + 1],
                                                       ALU.is_lt, ALU.mult)
                        dve.drain()
                        nc.vector.scalar_tensor_tensor(limit.bitcast(I32), turn, bit_next[:, i:i + 1],
                                                       limit.bitcast(I32), ALU.bitwise_xor, ALU.bitwise_xor)
                        dve.drain()

                def select(b):
                    s, m = scores[b % 2][:, 0:keys[b]], mask[:, b % 2, 0:keys[b]]
                    nc.vector.tensor_scalar(m, s, limit, 0.0, ALU.is_gt, ALU.add, accum_out=n_reach)
                    dve.drain()
                    nc.vector.scalar_tensor_tensor(s, s, limit, m, ALU.is_ge, ALU.add)
                    nc.vector.tensor_scalar(n_reach, n_reach, -float(TOPK), None, ALU.add)
                    dve.drain()
                    nc.vector.tensor_scalar(m, s, 1.0, None, ALU.is_equal)
                    dve.drain()
                    nc.vector.tensor_tensor(m[:, 0:1], m[:, 0:1], n_reach, ALU.add)
                    dve.drain()
                    nc.vector.tensor_tensor_scan(m, m, m, 0.0, ALU.add, ALU.add)
                    dve.drain()
                    nc.vector.scalar_tensor_tensor(s, m, 0.0, s, ALU.is_le, ALU.add)
                    dve.drain()
                    nc.vector.tensor_scalar(m, s, 2.0, NEG, ALU.is_lt, ALU.mult).then_inc(s_mask, 1)

                def logits(b, i):
                    n = HEADS * b + i
                    dve.wait_ge(s_qk, n + 1)
                    nc.vector.tensor_reduce(row_max, qk[:, 0:keys[b]], AX, ALU.max)
                    dve.drain()
                    wait(dve, s_exp, n - HEADS + 1)
                    nc.vector.tensor_scalar(n_max[:, i:i + 1], row_max, -SCALE, None, ALU.mult).then_inc(s_max, 1)

                def search_part(b, i):
                    if i == 0:
                        dve.wait_ge(s_causal, b - 1)
                    first = parts(b)[i - 1] if i else 0
                    if parts(b)[i] > first:
                        search(b, first, parts(b)[i])

                def inverse(b, g):
                    dve.wait_ge(s_exp, HEADS * b + REP * (g + 1))
                    wait(dve, s_rd, KV * b + g - 1)
                    nc.vector.reciprocal(inv_sum[:, g * REP:(g + 1) * REP], sums[:, g * REP:(g + 1) * REP]
                                         ).then_inc(s_inv, 1)

                def statistics(b):
                    dve.wait_ge(s_res, b + 1)
                    nc.vector.bn_stats(stats[:, 0:6], res[:, 0:512])
                    nc.vector.bn_stats(stats[:, 6:12], res[:, 512:1024])
                    dve.drain()
                    wait(dve, s_norm, b)
                    nc.vector.bn_aggr(mean_var, stats)
                    dve.drain()
                    nc.vector.tensor_scalar(var_eps, mean_var[:, 1:2], EPS, None, ALU.add).then_inc(s_var, 1)

                def choose(b):
                    dve.wait_ge(s_rl, b + 1)
                    nc.vector.tensor_tensor(r_logits[:], acc[:, 0:EXPERTS], b_router[:], ALU.add)
                    dve.drain()
                    wait(dve, s_eg, b)
                    nc.vector.max(best, r_logits[:])
                    dve.drain()
                    nc.vector.tensor_scalar(n_best, best[:, 0:1], -1.0, None, ALU.mult).then_inc(s_best, 1)
                    nc.vector.max_index(best_at[:], best, r_logits[:])
                    dve.drain()
                    nc.vector.tensor_copy(best_no[:], best_at[:])
                    dve.drain()
                    shape = [P, TOP_E, EXPERTS]
                    nc.vector.tensor_tensor(S["pick"][:, b], expert_no[:].unsqueeze(1).broadcast_to(shape),
                                            best_no[:, 0:TOP_E].unsqueeze(2).broadcast_to(shape), ALU.is_equal)
                    dve.drain()
                    wait(dve, s_cum, b)
                    wait(dve, s_rk, b)
                    nc.vector.tensor_reduce(chosen[:], S["pick"][:, b].rearrange("p k e -> p e k"), AX, ALU.add
                                            ).then_inc(s_ch, 1)

                def weigh(b):
                    dve.wait_ge(s_rks, b + 1)
                    nc.vector.scalar_tensor_tensor(r_logits[:], expert_no[:], float(SEQ), S["rank"][:, b],
                                                   ALU.mult, ALU.add)
                    dve.drain()
                    shape = [P, TOP_E, EXPERTS]
                    wide = pick_at[:].rearrange("p (k e) -> p k e", k=TOP_E)
                    nc.vector.tensor_tensor(wide, S["pick"][:, b], r_logits[:].unsqueeze(1).broadcast_to(shape), ALU.mult)
                    dve.drain()
                    nc.vector.tensor_reduce(at_f, wide, AX, ALU.add)
                    dve.drain()
                    wait(dve, s_list, 64 * b)
                    nc.vector.tensor_copy(at_i[:], at_f).then_inc(s_at, 1)
                    dve.wait_ge(s_eg, b + 1)
                    nc.vector.reciprocal(e_inv, e_sum)
                    dve.drain()
                    nc.vector.tensor_scalar(S["gates"][:, b], e_gate, e_inv, None, ALU.mult).then_inc(s_gate, 1)

                dve.wait_ge(s_const, CONSTS)
                dve.wait_ge(s_made, 4)
                walk({"logits": logits, "inverse": inverse, "choose": choose, "search": search_part, "select": select,
                      "statistics": statistics, "weigh": weigh})

            @block.tensor
            def _(pe):
                used = {}

                def claim(*names):
                    for n in names:
                        if used.get(n):
                            pe.wait_ge({"relu": s_relu, "pt": s_pts, "res": s_res, "ht": s_hts, "ov": s_ov,
                                        "sc": s_sc, "diff": s_diffs, "pools": s_pools, "best": s_best,
                                        "rk": s_rks}[n], used[n])

                PAIR = ("relu", "pt", "res", "ht", "ov")
                ACC = ("sc", "diff", "pools", "best", "rk")

                def score(b, c, head):
                    claim(*PAIR)
                    claim(*ACC)
                    if c == 0:
                        pe.wait_ge(s_iq[b % 2], 16 * ((b - 2) // 2 + 1))
                        pe.wait_ge(s_wd, b - 1)
                    u0 = IDX_H * (chunk0[b] + c)
                    at, width = c * BANK, min(BANK, keys[b] - c * BANK)
                    for i in range(IDX_H + 2):
                        if i < IDX_H:
                            row = slice(IDX_D * (i % 2), IDX_D * (i % 2 + 1))
                            wait(pe, s_relu, u0 + i - 1)
                            nc.tensor.matmul(pair[:, (u0 + i) % 2, 0:width], iq[row, b % 2, i // 2],
                                             S["ikT"][row, at:at + width], start=True, stop=True).then_inc(s_idx, 1)
                        if i >= 2:
                            j = i - 2
                            pe.wait_ge(s_relu, u0 + j + 1)
                            nc.tensor.matmul(acc[:, 0:width], w_diag[:, j], relu[:, (u0 + j) % 2, 0:width],
                                             start=(j == 0), stop=(j == IDX_H - 1)).then_inc(s_wsum, 1)
                    used["relu"] = u0 + IDX_H
                    used["sc"] = chunk0[b] + c + 1

                def logits(b, i):
                    n = HEADS * b + i
                    wait(pe, s_exp, n)
                    if i == 0:
                        pe.wait_ge(s_q[b % 2], 16 * (b // 2 + 1))
                        if b < 2:
                            pe.wait_ge(s_made, 4)
                        else:
                            pe.wait_ge(s_mask, b - 1)
                    for c in range(-(-keys[b] // BANK)):
                        at, width = c * BANK, min(BANK, keys[b] - c * BANK)
                        nc.tensor.matmul(qk[:, at:at + width], q[:, b % 2, i], S["kT"][:, i // REP, at:at + width],
                                         start=True, stop=False)
                        op = nc.tensor.matmul(qk[:, at:at + width], ident_bf[:], mask[:, b % 2, at:at + width],
                                              start=False, stop=True)
                    op.then_inc(s_qk, 1)

                def values(b, g, head):
                    n = KV * b + g
                    pe.wait_ge(s_exp, HEADS * b + REP * (g + 1))
                    claim(*PAIR)
                    wait(pe, s_ov, 2 * n)
                    v0 = pv0[b] + g * (b + 1)
                    for c in range(b + 2):
                        if c <= b:
                            wait(pe, s_pts, v0 + c - 1)
                            for j in range(REP):
                                slot = (HEADS * b + g * REP + j) % 4
                                op = nc.tensor.transpose(pair[:, (v0 + c) % 2, j * P:(j + 1) * P],
                                                         probs[:, slot, c * P:(c + 1) * P], S["ident"][:])
                            op.then_inc(s_pt, 1)
                        if c >= 1:
                            pe.wait_ge(s_pts, v0 + c)
                            nc.tensor.matmul(o_acc[:].rearrange("p a b -> p (a b)"),
                                             S["v"][:, c - 1, g * HEAD:(g + 1) * HEAD],
                                             probsT[:, (v0 + c - 1) % 2].rearrange("p a b -> p (a b)"),
                                             start=(c == 1), stop=(c == b + 1)).then_inc(s_pv, 1)
                    used["pt"] = v0 + b + 1
                    pe.wait_ge(s_rd, n + 1)
                    nc.tensor.matmul(pair[:, (v0 + b + 1) % 2, 0:REP * P], ones[:],
                                     r_diag[:].rearrange("p a b -> p (a b)"), start=True, stop=True).then_inc(s_ra, 1)
                    used["ov"] = 2 * n + 2

                def differ(b):
                    claim(*ACC)
                    if b == 0:
                        pe.wait_ge(s_const, CONSTS)
                    for g in range(POOL_GROUPS):
                        out = acc[POOL_G * (g % 2):POOL_G * (g % 2 + 1), (g // 2) * P:(g // 2 + 1) * P]
                        cols = slice(g * POOL_G, (g + 1) * POOL_G)
                        op = nc.tensor.matmul(out, S["u"][:, b, cols], band[:, 0 if b == 0 else 1, g],
                                              start=True, stop=(b == 0))
                        if b:
                            op = nc.tensor.matmul(out, S["u"][:, b - 1, cols], band[:, 2, g], start=False, stop=True)
                    op.then_inc(s_diff, 1)

                def pool(b):
                    pe.wait_ge(s_diffs, b + 1)
                    for c in range(2):
                        op = nc.tensor.matmul(acc[:, (2 + c) * P:(3 + c) * P], w_pool[:, c], diffT[:, c],
                                              start=True, stop=True)
                    op.then_inc(s_pool, 1)
                    used["pools"] = b + 1

                def project(b, head):
                    claim(*PAIR)
                    pe.wait_ge(s_mix, KV * (b + 1))
                    pe.wait_ge(s_pools, b + 1)
                    pe.wait_ge(s_hl, 16 * (b + 1))
                    for n in range(2):
                        for k in range(KD):
                            nc.tensor.matmul(pair[:, n], mixT[:, k], w_out[:, k, n * BANK:(n + 1) * BANK],
                                             start=(k == 0), stop=False)
                        op = nc.tensor.matmul(pair[:, n], alpha_ident[:], h[:, n * BANK:(n + 1) * BANK],
                                              start=False, stop=True)
                    op.then_inc(s_out, 1)
                    used["res"] = b + 1

                def transpose(b):
                    claim(*PAIR)
                    pe.wait_ge(s_h1, b + 1)
                    for n in range(2):
                        for j in range(4):
                            op = nc.tensor.transpose(pair[:, n, j * P:(j + 1) * P],
                                                     h1[:, (4 * n + j) * P:(4 * n + j + 1) * P], S["ident"][:])
                        op.then_inc(s_ht, 1)
                    used["ht"] = 2 * b + 2

                def route(b):
                    claim(*ACC)
                    pe.wait_ge(s_hts, 2 * b + 2)
                    for k in range(KD):
                        op = nc.tensor.matmul(acc[:, 0:EXPERTS], h1T[:, k], w_router[:, k],
                                              start=(k == 0), stop=(k == KD - 1))
                    op.then_inc(s_rl, 1)
                    used["best"] = b + 1

                def rank(b):
                    claim(*ACC)
                    pe.wait_ge(s_ch, b + 1)
                    wait(pe, s_cum, b)
                    nc.tensor.matmul(acc[:, 0:EXPERTS], before[:], chosen[:], start=True, stop=False)
                    nc.tensor.matmul(acc[:, 0:EXPERTS], ones[:], so_far[:], start=False, stop=True).then_inc(s_rk, 1)
                    used["rk"] = b + 1

                walk({"score": score, "logits": logits, "values": values, "differ": differ, "pool": pool,
                      "project": project, "transpose": transpose, "route": route, "rank": rank})

            @block.scalar
            def _(act):
                def score(b, c, head):
                    u0 = IDX_H * (chunk0[b] + c)
                    at, width = c * BANK, min(BANK, keys[b] - c * BANK)
                    for i in range(IDX_H):
                        if i == IDX_H * 3 // 4 and head:
                            exp(*head)
                        act.wait_ge(s_idx, u0 + i + 1)
                        wait(act, s_wsum, u0 + i - 1)
                        nc.scalar.activation(relu[:, (u0 + i) % 2, 0:width], pair[:, (u0 + i) % 2, 0:width],
                                             ACT.Relu).then_inc(s_relu, 1)
                    act.wait_ge(s_wsum, u0 + IDX_H)
                    if c == 0 and b >= 4:
                        act.wait_ge(s_mask, b - 3)
                    nc.scalar.activation(scores[b % 2][:, at:at + width], acc[:, 0:width], ACT.Copy).then_inc(s_sc, 1)

                def exp(b, i):
                    n = HEADS * b + i
                    act.wait_ge(s_max, n + 1)
                    g, j = divmod(n - 4, REP)
                    if n >= 4:
                        act.wait_ge(s_pt, pv0[g // 2] + (g % 2 + 1) * (g // 2 + 1))
                    if i == 0:
                        wait(act, s_inv, KV * b)
                    nc.scalar.activation(probs[:, n % 4, 0:keys[b]], qk[:, 0:keys[b]], ACT.Exp,
                                         bias=n_max[:, i:i + 1], scale=SCALE, accum_out=sums[:, i:i + 1]
                                         ).then_inc(s_exp, 1)

                def values(b, g, head):
                    n = KV * b + g
                    v0 = pv0[b] + g * (b + 1)
                    for c in range(b + 1):
                        if c == b * 3 // 4 and head:
                            exp(*head)
                        act.wait_ge(s_pt, v0 + c + 1)
                        wait(act, s_pv, v0 + c - 1)
                        nc.scalar.activation(probsT[:, (v0 + c) % 2].rearrange("p a b -> p (a b)"),
                                             pair[:, (v0 + c) % 2, 0:REP * P], ACT.Copy).then_inc(s_pts, 1)
                    act.wait_ge(s_pv, v0 + b + 1)
                    wait(act, s_mix, n)
                    nc.scalar.activation(oT[:], o_acc[:], ACT.Copy).then_inc(s_ov, 1)
                    act.wait_ge(s_ra, n + 1)
                    nc.scalar.activation(r_all[:].rearrange("p a b -> p (a b)"),
                                         pair[:, (v0 + b + 1) % 2, 0:REP * P], ACT.Copy).then_inc(s_ov, 1)

                def differ(b):
                    act.wait_ge(s_diff, b + 1)
                    act.wait_ge(s_mix, KV * b + 1)
                    nc.scalar.activation(diffT.rearrange("p a b -> p (a b)"), acc[:, 0:2 * P], ACT.Copy
                                         ).then_inc(s_diffs, 1)

                def pool(b):
                    act.wait_ge(s_pool, b + 1)
                    wait(act, s_out, b)
                    for c in range(2):
                        op = nc.scalar.activation(mixT[:, c], acc[:, (2 + c) * P:(3 + c) * P], ACT.Copy,
                                                  scale=pool_scale[:, c:c + 1])
                    op.then_inc(s_pools, 1)

                def project(b, head):
                    if head:
                        exp(*head)
                    act.wait_ge(s_out, b + 1)
                    wait(act, s_h1st, 16 * b)
                    wait(act, s_ht, 2 * b)
                    nc.scalar.activation(res[:], pair[:].rearrange("p a b -> p (a b)"), ACT.Copy).then_inc(s_res, 1)

                def norm(b):
                    act.wait_ge(s_rstd, b + 1)
                    nc.scalar.activation(h1[:], res[:], ACT.Identity, bias=shift, scale=rstd).then_inc(s_norm, 1)

                def transpose(b):
                    for n in range(2):
                        act.wait_ge(s_ht, 2 * b + n + 1)
                        wait(act, s_rl, b)
                        nc.scalar.activation(h1T[:, 4 * n:4 * n + 4].rearrange("p a b -> p (a b)"), pair[:, n],
                                             ACT.Copy).then_inc(s_hts, 1)

                def gate(b):
                    act.wait_ge(s_best, b + 1)
                    wait(act, s_gate, b)
                    nc.scalar.activation(e_gate, best[:, 0:TOP_E], ACT.Exp, bias=n_best, accum_out=e_sum
                                         ).then_inc(s_eg, 1)

                def rank(b):
                    gate(b)
                    act.wait_ge(s_rk, b + 1)
                    nc.scalar.activation(S["rank"][:, b], acc[:, 0:EXPERTS], ACT.Copy).then_inc(s_rks, 1)

                act.wait_ge(s_const, CONSTS)
                act.wait_ge(s_clear, CLEARS)
                walk({"score": score, "exp": exp, "values": values, "differ": differ, "pool": pool,
                      "project": project, "norm": norm, "transpose": transpose, "rank": rank})


def place_stage(nc, A, S, D_):
    with ExitStack() as ctx:
        def sb(name, shape, dt=F32):
            return ctx.enter_context(nc.sbuf_tensor(name, shape, dt))

        ones = sb("ones_p", [P, P])
        visit_no = sb("visit_no", [P, META])
        expert_no = sb("expert_no_p", [P, EXPERTS])
        b_rows = sb("b_rows", [EXPERTS, 2 * FF])
        counts = sb("counts", [P, EXPERTS])
        blocks_i = sb("blocks_i", [P, EXPERTS], I32)
        thirds_i = sb("thirds_i", [P, EXPERTS], I32)
        visits = sb("visits", [P, EXPERTS])
        until = sb("until", [P, EXPERTS])
        first = sb("first", [P, EXPERTS])
        row0 = sb("row0", [P, EXPERTS])
        row = sb("row", [P, TILES, EXPERTS])
        wide = sb("wide", [P, TILES, TOP_E, EXPERTS])
        pos_f = sb("place_f", [P, TILES, TOP_E])
        over = sb("over", [P, META, EXPERTS])
        whose = sb("whose", [P, META])
        nth = sb("nth", [P, META])
        left = sb("left", [P, META])
        start = sb("start", [P, META])
        more_f = sb("more_f", [P, 1])
        count = ctx.enter_context(nc.psum_tensor("count", [P, BANK], F32))
        turned = ctx.enter_context(nc.psum_tensor("turned", [P, 2 * FF // P, EXPERTS], F32))
        s_made = ctx.enter_context(nc.semaphore("l_made"))
        s_bias = ctx.enter_context(nc.semaphore("l_bias"))
        s_count = ctx.enter_context(nc.semaphore("l_count"))
        s_turn = ctx.enter_context(nc.semaphore("l_turn"))

        with nc.Block() as block:
            @block.sync
            def _(sp):
                sp.dma_start(b_rows[:], A["b_gate_up"][0]).then_inc(s_bias, 16)

            @block.gpsimd
            def _(pool):
                nc.gpsimd.memset(ones[:], 1.0).then_inc(s_made, 1)
                nc.gpsimd.iota(expert_no[:], pattern=[[1, EXPERTS]], base=0, channel_multiplier=0,
                               allow_small_or_imprecise_dtypes=True).then_inc(s_made, 1)
                nc.gpsimd.iota(visit_no[:], pattern=[[1, META]], base=0, channel_multiplier=0,
                               allow_small_or_imprecise_dtypes=True).then_inc(s_made, 1)

            @block.tensor
            def _(pe):
                pe.wait_ge(s_made, 1)
                nc.tensor.matmul(count[:, 0:EXPERTS], ones[:], S["so_far"][:], start=True, stop=True
                                 ).then_inc(s_count, 1)
                pe.wait_ge(s_bias, 16)
                for j in range(2 * FF // P):
                    op = nc.tensor.transpose(turned[:, j], b_rows[:, j * P:(j + 1) * P],
                                             S["ident"][0:EXPERTS, 0:EXPERTS])
                op.then_inc(s_turn, 1)

            @block.scalar
            def _(act):
                act.wait_ge(s_turn, 1)
                nc.scalar.activation(S["b_gu"][:], turned[:], ACT.Copy)

            @block.vector
            def _(dve):
                dve.wait_ge(s_made, 3)
                dve.wait_ge(s_count, 1)
                nc.vector.tensor_copy(counts[:], count[:, 0:EXPERTS])
                dve.drain()
                nc.vector.tensor_scalar(blocks_i[:], counts[:], float(ROWS - 1), None, ALU.add)
                dve.drain()
                nc.vector.tensor_scalar(blocks_i[:], blocks_i[:], 7, None, ALU.logical_shift_right)
                dve.drain()
                nc.vector.tensor_scalar(thirds_i[:], blocks_i[:], 171.0, None, ALU.mult)
                dve.drain()
                nc.vector.tensor_scalar(thirds_i[:], thirds_i[:], 9, None, ALU.logical_shift_right)
                dve.drain()
                nc.vector.tensor_scalar(visits[:], thirds_i[:], 1.0, None, ALU.max)
                nc.vector.memset(first[:], 1.0)
                dve.drain()
                nc.vector.tensor_tensor_scan(until[:], first[:], visits[:], 0.0, ALU.mult, ALU.add)
                dve.drain()
                nc.vector.tensor_tensor(first[:], until[:], visits[:], ALU.subtract)
                nc.vector.tensor_scalar(S["more"][:], until[:, EXPERTS - 1:EXPERTS], -1.0, None, ALU.add)
                dve.drain()
                nc.vector.tensor_scalar(row0[:], first[:], float(ROWS), None, ALU.mult)
                dve.drain()
                shape = [P, TILES, EXPERTS]
                nc.vector.tensor_tensor(row[:], S["rank"][:], row0[:].unsqueeze(1).broadcast_to(shape), ALU.add)
                dve.drain()
                shape = [P, TILES, TOP_E, EXPERTS]
                nc.vector.tensor_tensor(wide[:], S["pick"][:], row[:].unsqueeze(2).broadcast_to(shape), ALU.mult)
                dve.drain()
                nc.vector.tensor_reduce(pos_f[:], wide[:], AX, ALU.add)
                shape = [P, META, EXPERTS]
                nc.vector.tensor_tensor(over[:], until[:].unsqueeze(1).broadcast_to(shape),
                                        visit_no[:].unsqueeze(2).broadcast_to(shape), ALU.is_le)
                dve.drain()
                nc.vector.tensor_copy(S["pos"][:], pos_f[:])
                nc.vector.tensor_reduce(whose[:], over[:], AX, ALU.add)
                dve.drain()
                nc.vector.tensor_scalar(whose[:], whose[:], float(EXPERTS - 1), None, ALU.min)
                dve.drain()
                nc.vector.tensor_copy(S["meta"][:, :, 0], whose[:])
                for out, table in ((nth, first), (left, counts)):
                    nc.vector.tensor_tensor(over[:], expert_no[:].unsqueeze(1).broadcast_to(shape),
                                            whose[:].unsqueeze(2).broadcast_to(shape), ALU.is_equal)
                    dve.drain()
                    nc.vector.tensor_tensor(over[:], over[:], table[:].unsqueeze(1).broadcast_to(shape), ALU.mult)
                    dve.drain()
                    nc.vector.tensor_reduce(out[:], over[:], AX, ALU.add)
                    dve.drain()
                nc.vector.tensor_tensor(nth[:], visit_no[:], nth[:], ALU.subtract)
                dve.drain()
                nc.vector.scalar_tensor_tensor(left[:], nth[:], -float(ROWS), left[:], ALU.mult, ALU.add)
                nc.vector.tensor_scalar(nth[:], nth[:], float(ROWS), None, ALU.mult)
                dve.drain()
                nc.vector.scalar_tensor_tensor(start[:], whose[:], float(SEQ), nth[:], ALU.mult, ALU.add)
                dve.drain()
                nc.vector.tensor_copy(S["meta"][:, :, 1], start[:])
                dve.drain()
                nc.vector.tensor_scalar(start[:], left[:], float(WIDTHS[0]), None, ALU.is_gt)
                nc.vector.tensor_scalar(nth[:], left[:], float(WIDTHS[1]), None, ALU.is_gt)
                dve.drain()
                nc.vector.tensor_tensor(S["meta"][:, :, 2], start[:], nth[:], ALU.add)


def experts_stage(nc, A, S, D_):
    with ExitStack() as ctx:
        def sb(name, shape, dt=F32):
            return ctx.enter_context(nc.sbuf_tensor(name, shape, dt))

        def sem(name):
            return ctx.enter_context(nc.semaphore(name))

        raw = sb("w_raw", [P, 3, CHUNK])
        w_hi = sb("w_hi", [P, 2, CHUNK], F32R)
        w_lo = sb("w_lo", [P, 2, CHUNK], F32R)
        who = sb("who", [P, 3], I32)
        who_now = sb("who_now", [P, 3], I32)
        zero = sb("zero", [P, 3], I32)
        x = sb("x_rows", [P, 3, D])
        x_hi = sb("x_hi", [P, KD, ROWS], F32R)
        x_lo = sb("x_lo", [P, KD, ROWS], F32R)
        gate = sb("gate", [P, 2, ROWS])
        up = sb("up", [P, 2, ROWS])
        sig = sb("sig", [P, 2, ROWS])
        a_hi = sb("a_hi", [P, FF // P, ROWS], F32R)
        a_lo = sb("a_lo", [P, FF // P, ROWS], F32R)
        y = sb("y_rows", [P, 2, BANK])
        gu = ctx.enter_context(nc.psum_tensor("gu", [P, 2, 2, BANK], F32))
        tr = ctx.enter_context(nc.psum_tensor("e_tr", [P, 2, BANK], F32))
        yp = ctx.enter_context(nc.psum_tensor("yp", [P, 2, BANK], F32))

        s_clear = sem("e_clear")
        s_raw = [sem(f"e_raw{n}") for n in range(3)]
        s_hi = sem("e_hi")
        s_lo = sem("e_lo")
        s_who = sem("e_who")
        s_x = sem("e_x")
        s_xt = sem("e_xt")
        s_xh = sem("e_xh")
        s_xl = sem("e_xl")
        s_g1 = sem("e_g1")
        s_gm = sem("e_gm")
        s_gu = sem("e_gu")
        s_sig = sem("e_sig")
        s_act = sem("e_act")
        s_ah = sem("e_ah")
        s_al = sem("e_al")
        s_g2 = sem("e_g2")
        s_y = sem("e_y")
        s_yst = [sem("e_yst0"), sem("e_yst1")]

        J = FF // P

        def over_visits(eng, body):
            more = eng.value_load(S["more"][0:1, 0:1], min_val=EXPERTS - 1, max_val=MAX_VISITS - 1)
            body(0)
            with eng.Fori(1, more + 1) as v:
                body(v)
            return more + 1

        def look_up(eng, v, what, most):
            return eng.value_load(S["meta"][0:1, slice(v, v + 1) if isinstance(v, int) else bass.ds(v, 1), what],
                                  min_val=0, max_val=most)

        def first(v):
            return isinstance(v, int) and v == 0

        with nc.Block() as block:
            @block.sync
            def _(sp):
                w_gu, w_d = A["w_gate_up"][0], A["w_down"][0]

                def chunk(v, c, e):
                    if not first(v) or c >= 3:
                        sp.wait_ge(s_lo, 12 * v + 2 * (c - 3) + 2)
                    out = raw[:, c % 3]
                    if c < 4:
                        src = w_gu[bass.ds(e, 1)].rearrange("o (k p) n -> (o p) k n", p=P)
                        for h in range(2):
                            at = h * FF + c * 256
                            sp.dma_start(out.rearrange("p (k h n) -> p k h n", k=KD, h=2)[:, :, h],
                                         src[:, :, at:at + 256]).then_inc(s_raw[c % 3], 16)
                    else:
                        src = w_d[bass.ds(e, 1)].rearrange("o (k p) n -> (o p) k n", p=P)
                        for h in range(2):
                            sp.dma_start(out.rearrange("p (k n) -> p k n", k=KD)[:, 4 * h:4 * h + 4],
                                         src[:, 4 * h:4 * h + 4, (c - 4) * BANK:(c - 3) * BANK]
                                         ).then_inc(s_raw[c % 3], 16)

                def body(v):
                    e = look_up(sp, v, 0, EXPERTS - 1)
                    for c in range(6):
                        chunk(v, c, e)

                n = over_visits(sp, body)
                chunk(n, 0, look_up(sp, n, 0, EXPERTS - 1))

            @block.gpsimd
            def _(pool):
                def gather(v):
                    at = look_up(pool, v, 1, (EXPERTS - 1) * SEQ + 6 * ROWS)
                    if not first(v):
                        pool.wait_ge(s_x, 48 * v)
                        pool.wait_ge(s_xt, 8 * v)
                    nc.gpsimd.dma_start(who[:], D_["lists"][bass.ds(at, ROWS), :].rearrange(
                        "(m p) o -> p (m o)", p=P), allow_slow_non_contiguous=True).then_inc(s_who, 16)
                    pool.wait_ge(s_who, 16 * v + 16)
                    nc.gpsimd.tensor_tensor(who_now[:], who[:], zero[:], ALU.add)
                    pool.drain()
                    for m in range(3):
                        nc.gpsimd.indirect_dma_start(
                            x[:, m], None, D_["h1"], bass.IndirectOffsetOnAxis(ap=who_now[:, m:m + 1], axis=0)
                        ).then_inc(s_x, 16)

                def body(v):
                    gather(v + 1)
                    for j in range(J):
                        pool.wait_ge(s_ah, 8 * v + j + 1)
                        nc.gpsimd.tensor_tensor(a_lo[:, j], up[:, j % 2], a_hi[:, j].bitcast(F32), ALU.subtract
                                                ).then_inc(s_al, 1)

                nc.gpsimd.memset(zero[:], 0)
                pool.drain()
                gather(0)
                n = over_visits(pool, body)
                pool.wait_ge(s_x, 48 * n + 48)
                nc.gpsimd.tensor_tensor(who_now[:], who[:], zero[:], ALU.add)

            @block.tensor
            def _(pe):
                def transpose_x(v, k):
                    if k == 0:
                        pe.wait_ge(s_x, 48 * v + 48)
                    if not first(v) or k >= 2:
                        pe.wait_ge(s_xl, 8 * v + k - 1)
                    for m in range(3):
                        op = nc.tensor.transpose(tr[:, k % 2, m * P:(m + 1) * P], x[:, m, k * P:(k + 1) * P],
                                                 S["ident"][:])
                    op.then_inc(s_xt, 1)

                def passes(out, pairs, ready=None):
                    for n, (s_hi_, s_lo_, m_hi, m_lo) in enumerate(pairs):
                        if ready is not None:
                            pe.wait_ge(s_al, ready + n + 1)
                        nc.tensor.matmul(out, s_hi_, m_hi, start=(n == 0), stop=False)
                        nc.tensor.matmul(out, s_hi_, m_lo, start=False, stop=False)
                        op = nc.tensor.matmul(out, s_lo_, m_hi, start=False, stop=(n == len(pairs) - 1))
                    return op

                def up_chunk(v, c, width):
                    hi, lo = (w[:, c % 2].rearrange("p (k h n) -> p k h n", k=KD, h=2) for w in (w_hi, w_lo))
                    for jj in range(2):
                        j = 2 * c + jj
                        if not first(v) or j >= 2:
                            pe.wait_ge(s_gu, 8 * v + j - 1)
                        for h in range(2):
                            cols = slice(jj * P, (jj + 1) * P)
                            op = passes(gu[:, j % 2, h, 0:width],
                                        [(hi[:, k, h, cols], lo[:, k, h, cols], x_hi[:, k, 0:width], x_lo[:, k, 0:width])
                                         for k in range(KD)])
                        op.then_inc(s_g1, 1)

                def down_tile(v, c, m):
                    hi, lo = (w[:, c % 2].rearrange("p (k n) -> p k n", k=KD) for w in (w_hi, w_lo))
                    n = 3 * (c - 4) + m
                    rows = slice(m * P, (m + 1) * P)
                    return passes(yp[:, n % 2], [(a_hi[:, k, rows], a_lo[:, k, rows], hi[:, k], lo[:, k])
                                                 for k in range(KD)], 8 * v if n == 0 else None)

                def body(v):
                    kind = look_up(pe, v, 2, 2)
                    for c in range(4):
                        pe.wait_ge(s_lo, 12 * v + 2 * c + 2)
                        if c == 0:
                            pe.wait_ge(s_xl, 8 * v + 8)
                        for n, width in enumerate(WIDTHS):
                            with pe.If(kind == n):
                                up_chunk(v, c, width)
                    transpose_x(v + 1, 0)
                    transpose_x(v + 1, 1)
                    for c in (4, 5):
                        pe.wait_ge(s_lo, 12 * v + 2 * c + 2)
                        for m in range(3):
                            n = 3 * (c - 4) + m
                            if not first(v) or n >= 2:
                                pe.wait_ge(s_y, 6 * v + n - 1)
                            if m < 2:
                                down_tile(v, c, m).then_inc(s_g2, 1)
                            else:
                                with pe.If(kind != 0):
                                    down_tile(v, c, m).then_inc(s_g2, 1)
                                with pe.Else():
                                    nc.tensor.matmul(yp[:, n % 2, 0:EXPERTS], S["ident"][:], S["so_far"][:],
                                                     start=True, stop=True).then_inc(s_g2, 1)
                            if n in (0, 1, 3, 4):
                                at = 2 + 2 * (0, 1, 3, 4).index(n)
                                if at < KD:
                                    transpose_x(v + 1, at)
                                    transpose_x(v + 1, at + 1)

                pe.wait_ge(s_clear, 1)
                for k in range(KD):
                    transpose_x(0, k)
                over_visits(pe, body)

            @block.vector
            def _(dve):
                def low(v, c, half):
                    n = 12 * v + 2 * c + half
                    dve.wait_ge(s_hi, n + 1)
                    cols = slice(half * CHUNK // 2, (half + 1) * CHUNK // 2)
                    nc.vector.tensor_tensor(w_lo[:, c % 2, cols], raw[:, c % 3, cols],
                                            w_hi[:, c % 2, cols].bitcast(F32), ALU.subtract).then_inc(s_lo, 1)

                def low_x(v, k):
                    dve.wait_ge(s_xh, 8 * v + k + 1)
                    nc.vector.tensor_tensor(x_lo[:, k], tr[:, k % 2, 0:ROWS], x_hi[:, k].bitcast(F32), ALU.subtract
                                            ).then_inc(s_xl, 1)

                def out_of_psum(v, j, e):
                    g, u = gate[:, j % 2], up[:, j % 2]
                    dve.wait_ge(s_g1, 8 * v + j + 1)
                    nc.vector.tensor_scalar(g, gu[:, j % 2, 0, 0:ROWS], S["b_gu"][:, j, bass.ds(e, 1)], LIMIT,
                                            ALU.add, ALU.min).then_inc(s_gm, 1)
                    if not first(v) or j >= 2:
                        dve.wait_ge(s_al, 8 * v + j - 1)
                    nc.vector.tensor_scalar(u, gu[:, j % 2, 1, 0:ROWS], S["b_gu"][:, J + j, bass.ds(e, 1)], LIMIT,
                                            ALU.add, ALU.min).then_inc(s_gu, 1)
                    dve.drain()
                    nc.vector.tensor_scalar(u, u, -LIMIT, 1.0, ALU.max, ALU.add)
                    dve.drain()
                    nc.vector.tensor_tensor(u, u, g, ALU.mult)

                def activate(v, j):
                    u = up[:, j % 2]
                    dve.drain()
                    dve.wait_ge(s_sig, 8 * v + j + 1)
                    nc.vector.tensor_tensor(u, u, sig[:, j % 2], ALU.mult).then_inc(s_act, 1)

                def body(v):
                    e = look_up(dve, v, 0, EXPERTS - 1)
                    for c in range(4):
                        if c:
                            out_of_psum(v, 2 * c - 1, e)
                        low(v, c + 1, 0)
                        if c:
                            activate(v, 2 * c - 1)
                        low(v, c + 1, 1)
                        out_of_psum(v, 2 * c, e)
                        activate(v, 2 * c)
                    out_of_psum(v, J - 1, e)
                    low_x(v + 1, 0)
                    activate(v, J - 1)
                    low_x(v + 1, 1)
                    low(v, 5, 0)
                    low(v, 5, 1)
                    for k in range(2, 6):
                        low_x(v + 1, k)
                    low(v + 1, 0, 0)
                    low(v + 1, 0, 1)
                    low_x(v + 1, 6)
                    low_x(v + 1, 7)

                for bank in (gu, yp):
                    nc.vector.memset(bank[:], 0.0)
                dve.drain()
                nc.vector.memset(tr[:], 0.0).then_inc(s_clear, 1)
                low(0, 0, 0)
                low(0, 0, 1)
                for k in range(KD):
                    low_x(0, k)
                over_visits(dve, body)

            @block.scalar
            def _(act):
                def high(v, c, half):
                    n = 12 * v + 2 * c + half
                    if half == 0:
                        act.wait_ge(s_raw[c % 3], 64 * v + 32 * (c // 3) + 32)
                        if c >= 2 and c < 6:
                            act.wait_ge(s_g1, 8 * v + 2 * (c - 2) + 2)
                        elif not first(v):
                            act.wait_ge(s_g2, 6 * v - 3 + 3 * c)
                    cols = slice(half * CHUNK // 2, (half + 1) * CHUNK // 2)
                    nc.scalar.activation(w_hi[:, c % 2, cols], raw[:, c % 3, cols], ACT.Copy).then_inc(s_hi, 1)

                def high_x(v, k):
                    act.wait_ge(s_xt, 8 * v + k + 1)
                    nc.scalar.activation(x_hi[:, k], tr[:, k % 2, 0:ROWS], ACT.Copy).then_inc(s_xh, 1)

                def sigmoid(v, j):
                    act.wait_ge(s_gm, 8 * v + j + 1)
                    nc.scalar.activation(sig[:, j % 2], gate[:, j % 2], ACT.Sigmoid, scale=SWI_ALPHA).then_inc(s_sig, 1)

                def high_act(v, j):
                    act.wait_ge(s_act, 8 * v + j + 1)
                    nc.scalar.activation(a_hi[:, j], up[:, j % 2], ACT.Copy).then_inc(s_ah, 1)

                def store(v, n):
                    slot = n % 2
                    act.wait_ge(s_g2, 6 * v + n + 1)
                    if not first(v) or n >= 2:
                        act.wait_ge(s_yst[slot], 48 * v + 16 * (n // 2))
                    nc.scalar.activation(y[:, slot], yp[:, slot], ACT.Copy).then_inc(s_y, 1)
                    act.wait_ge(s_y, 6 * v + n + 1)
                    nc.scalar.dma_start(
                        D_["y"][bass.ds(v * ROWS + (n % 3) * P, P), (n // 3) * BANK:(n // 3 + 1) * BANK], y[:, slot]
                    ).then_inc(s_yst[slot], 16)

                def body(v):
                    for c in range(4):
                        high(v, c + 1, 0)
                        if c:
                            sigmoid(v, 2 * c - 1)
                        high(v, c + 1, 1)
                        if c:
                            high_act(v, 2 * c - 1)
                        sigmoid(v, 2 * c)
                        high_act(v, 2 * c)
                    high_x(v + 1, 0)
                    sigmoid(v, J - 1)
                    high_x(v + 1, 1)
                    high_act(v, J - 1)
                    high(v, 5, 0)
                    high(v, 5, 1)
                    k = 2
                    for n in range(6):
                        store(v, n)
                        if n in (0, 1, 3):
                            high_x(v + 1, k)
                            high_x(v + 1, k + 1)
                            k += 2
                        if n == 2:
                            high(v + 1, 0, 0)
                            high(v + 1, 0, 1)

                high(0, 0, 0)
                high(0, 0, 1)
                for k in range(KD):
                    high_x(0, k)
                n = over_visits(act, body)
                act.wait_ge(s_yst[0], 48 * n)
                act.wait_ge(s_yst[1], 48 * n)
                nc.scalar.activation(y[:, 0, 0:1], y[:, 0, 0:1], ACT.Copy)


def combine_stage(nc, A, S, D_):
    with ExitStack() as ctx:
        def sb(name, shape, dt=F32):
            return ctx.enter_context(nc.sbuf_tensor(name, shape, dt))

        def sem(name):
            return ctx.enter_context(nc.semaphore(name))

        gain = sb("gain_2", [P, D])
        bias = sb("bias_2", [P, D])
        b_down = sb("b_down_sb", [EXPERTS, D])
        at = sb("at", [P, 2, TOP_E], I32)
        g_now = sb("g_now", [P, TOP_E])
        rows = sb("rows", [P, 2, TOP_E, D])
        h1 = sb("h1_blk", [P, 2, D])
        alpha_ident = sb("alpha_ident2", [P, P])
        g_diag = sb("g_diag", [P, 2, TOP_E, P])
        by_pick = sb("by_pick", [P, TOP_E, EXPERTS])
        by_expert = sb("by_expert", [P, 2, EXPERTS])
        by_expertT = sb("by_expertT", [EXPERTS, P])
        total = sb("total", [P, 2, D])
        out = sb("out_blk", [P, 2, D])
        small = sb("small2", [P, 2, 32])
        minus_half = sb("minus_half2", [P, 1])
        acc = ctx.enter_context(nc.psum_tensor("c_acc", [P, 2, D], F32))
        trp = ctx.enter_context(nc.psum_tensor("c_tr", [P, BANK], F32))

        s_const = sem("c_const")
        s_made = sem("c_made")
        s_h1 = [sem("c_h10"), sem("c_h11")]
        s_rows = [sem("c_rows0"), sem("c_rows1")]
        s_by = sem("c_by")
        s_gd = sem("c_gd")
        s_bt = sem("c_bt")
        s_bts = sem("c_bts")
        s_sum = sem("c_sum")
        s_tot = sem("c_tot")
        s_var = sem("c_var")
        s_rstd = sem("c_rstd")
        s_norm = sem("c_norm")
        s_out = sem("c_out")
        s_st = [sem("c_st0"), sem("c_st1")]

        def pairs(eng, body):
            for t in range(4):
                body(t, t % 2, t // 2)
            with eng.Fori(2, TILES // 2) as i:
                body(2 * i, 0, i)
                body(2 * i + 1, 1, i)

        def cut(t):
            return slice(t * P, t * P + P) if isinstance(t, int) else bass.ds(t * P, P)

        out_dram = A["out"].rearrange("b s d -> (b s) d")

        with nc.Block() as block:
            @block.sync
            def _(sp):
                sp.dma_start(b_down[:], A["b_down"][0]).then_inc(s_const, 16)
                sp.dma_start(gain[:], A["ln2_g"][0].partition_broadcast(P)).then_inc(s_const, 16)
                sp.dma_start(bias[:], A["ln2_b"][0].partition_broadcast(P)).then_inc(s_const, 16)

                def body(t, slot, half):
                    wait(sp, s_sum, t - 1)
                    sp.dma_start(h1[:, slot], D_["h1"][cut(t), :]).then_inc(s_h1[slot], 16)

                pairs(sp, body)

            @block.gpsimd
            def _(pool):
                nc.gpsimd.tensor_scalar(alpha_ident[:], S["ident"][:], ALPHA_RES, 1.0, ALU.mult, ALU.mult
                                        ).then_inc(s_made, 1)
                nc.gpsimd.memset(minus_half[:], -0.5).then_inc(s_made, 1)

                def gather(t, slot, half):
                    wait(pool, s_sum, t - 1)
                    if not isinstance(t, int) or t >= 2:
                        pool.wait_ge(s_rows[slot], 64 * half)
                    nc.gpsimd.tensor_copy(at[:, slot], S["pos"][:, t])
                    nc.gpsimd.tensor_copy(g_now[:], S["gates"][:, t])
                    pool.drain()
                    for k in range(TOP_E):
                        op = nc.gpsimd.tensor_scalar(g_diag[:, slot, k], S["ident"][:], g_now[:, k:k + 1], 1.0,
                                                     ALU.mult, ALU.mult)
                    op.then_inc(s_gd, 1)
                    pool.drain()
                    for k in range(TOP_E):
                        nc.gpsimd.indirect_dma_start(
                            rows[:, slot, k], None, D_["y"], bass.IndirectOffsetOnAxis(ap=at[:, slot, k:k + 1], axis=0)
                        ).then_inc(s_rows[slot], 16)

                def power(t, slot):
                    var_eps, rstd = small[:, slot, 14:15], small[:, slot, 15:16]
                    pool.wait_ge(s_var, t + 1)
                    nc.gpsimd.tensor_tensor(rstd, var_eps, minus_half[:], ALU.pow).then_inc(s_rstd, 1)

                def finish(t, slot):
                    pool.wait_ge(s_norm, t + 1)
                    nc.gpsimd.tensor_tensor(out[:, slot], out[:, slot], bias[:], ALU.add).then_inc(s_out, 1)

                pool.wait_ge(s_made, 2)
                pool.wait_ge(s_const, 48)
                gather(0, 0, 0)
                gather(1, 1, 0)

                def body(t, slot, half):
                    power(t, slot)
                    gather(t + 2, slot, half + 1)
                    finish(t, slot)

                for t in range(4):
                    body(t, t % 2, t // 2)
                with pool.Fori(2, TILES // 2 - 1) as i:
                    body(2 * i, 0, i)
                    body(2 * i + 1, 1, i)
                for t in (TILES - 2, TILES - 1):
                    power(t, t % 2)
                    finish(t, t % 2)

            @block.tensor
            def _(pe):
                pe.wait_ge(s_const, 48)
                pe.wait_ge(s_made, 2)

                def body(t, slot, half):
                    pe.wait_ge(s_h1[slot], 16 * (half + 1))
                    wait(pe, s_tot, t - 1)
                    pe.wait_ge(s_gd, t + 1)
                    for n in range(2):
                        cols = slice(n * BANK, (n + 1) * BANK)
                        nc.tensor.matmul(acc[:, slot, cols], alpha_ident[:], h1[:, slot, cols], start=True, stop=False)
                    pe.wait_ge(s_rows[slot], 64 * (half + 1))
                    for n in range(2):
                        cols = slice(n * BANK, (n + 1) * BANK)
                        for k in range(TOP_E):
                            nc.tensor.matmul(acc[:, slot, cols], g_diag[:, slot, k], rows[:, slot, k, cols],
                                             start=False, stop=False)
                        if n == 0:
                            pe.wait_ge(s_by, t + 1)
                            wait(pe, s_bts, t)
                            nc.tensor.transpose(trp[0:EXPERTS, 0:P], by_expert[:, slot], S["ident"][:]
                                                ).then_inc(s_bt, 1)
                    pe.wait_ge(s_bts, t + 1)
                    for n in range(2):
                        cols = slice(n * BANK, (n + 1) * BANK)
                        op = nc.tensor.matmul(acc[:, slot, cols], by_expertT[:], b_down[:, cols],
                                              start=False, stop=True)
                    op.then_inc(s_sum, 1)

                pairs(pe, body)

            @block.vector
            def _(dve):
                def gates(t, slot):
                    shape = [P, TOP_E, EXPERTS]
                    nc.vector.tensor_tensor(by_pick[:], S["pick"][:, t],
                                            S["gates"][:, t].unsqueeze(2).broadcast_to(shape), ALU.mult)
                    dve.drain()
                    wait(dve, s_bt, t - 1)
                    nc.vector.tensor_reduce(by_expert[:, slot], by_pick[:].rearrange("p k e -> p e k"), AX, ALU.add
                                            ).then_inc(s_by, 1)

                def body(t, slot, half):
                    gates(t, slot)
                    stats, mean_var = small[:, slot, 0:12], small[:, slot, 12:14]
                    var_eps, rstd = small[:, slot, 14:15], small[:, slot, 15:16]
                    dve.wait_ge(s_tot, t + 1)
                    nc.vector.bn_stats(stats[:, 0:6], total[:, slot, 0:512])
                    nc.vector.bn_stats(stats[:, 6:12], total[:, slot, 512:1024])
                    dve.drain()
                    nc.vector.bn_aggr(mean_var, stats)
                    dve.drain()
                    nc.vector.tensor_scalar(var_eps, mean_var[:, 1:2], EPS, None, ALU.add).then_inc(s_var, 1)
                    dve.wait_ge(s_rstd, t + 1)
                    if not isinstance(t, int) or t >= 2:
                        dve.wait_ge(s_st[slot], 16 * half)
                    nc.vector.tensor_scalar(out[:, slot], total[:, slot], mean_var[:, 0:1], rstd,
                                            ALU.subtract, ALU.mult)
                    dve.drain()
                    nc.vector.tensor_tensor(out[:, slot], out[:, slot], gain[:], ALU.mult).then_inc(s_norm, 1)

                dve.wait_ge(s_const, 48)
                pairs(dve, body)

            @block.scalar
            def _(act):
                def body(t, slot, half):
                    act.wait_ge(s_bt, t + 1)
                    wait(act, s_sum, t)
                    nc.scalar.activation(by_expertT[:], trp[0:EXPERTS, 0:P], ACT.Copy).then_inc(s_bts, 1)
                    act.wait_ge(s_sum, t + 1)
                    wait(act, s_norm, t - 1)
                    nc.scalar.activation(total[:, slot], acc[:, slot], ACT.Copy).then_inc(s_tot, 1)

                def store(t, slot):
                    act.wait_ge(s_out, t + 1)
                    nc.scalar.dma_start(out_dram[cut(t), :], out[:, slot]).then_inc(s_st[slot], 16)

                def both(t, slot, half):
                    body(t, slot, half)
                    if not isinstance(t, int) or t >= 1:
                        store(t - 1, 1 - slot)

                pairs(act, both)
                store(TILES - 1, 1)
                act.wait_ge(s_st[0], 8 * TILES)
                act.wait_ge(s_st[1], 8 * TILES)


def build(nc, A, upto=9):
    with ExitStack() as ctx:
        def sb(name, shape, dt=F32):
            return ctx.enter_context(nc.sbuf_tensor(name, shape, dt))
        S = {"ident": sb("ident", [P, P]),
             "pick": sb("pick", [P, TILES, TOP_E, EXPERTS], BF16),
             "rank": sb("rank", [P, TILES, EXPERTS]),
             "gates": sb("gates", [P, TILES, TOP_E]),
             "so_far": sb("so_far", [P, EXPERTS])}
        D_ = {"x": A["x"].rearrange("b s d -> (b s) d"),
              "h": nc.dram_tensor("h_dram", (SEQ, D), F32).ap(),
              "h1": nc.dram_tensor("h1_dram", (SEQ, D), F32).ap(),
              "lists": nc.dram_tensor("lists_dram", (EXPERTS * SEQ + TAIL, 1), I32).ap(),
              "y": nc.dram_tensor("y_dram", (MAX_VISITS * ROWS, D), F32).ap(),
              "qi": nc.dram_tensor("qi_dram", (SEQ, NQI * P), F32).ap()}
        with ExitStack() as c2:
            def sb2(name, shape, dt=F32):
                return c2.enter_context(nc.sbuf_tensor(name, shape, dt))
            S["kT"] = sb2("kT", [P, KV, SEQ])
            S["ikT"] = sb2("ikT", [P, SEQ])
            S["v"] = sb2("v_sb", [P, TILES, KV * HEAD])
            S["u"] = sb2("u_sb", [P, TILES, POOL_W])
            S["iw"] = sb2("iw_sb", [P, TILES, IDX_H])
            project_stage(nc, A, S, D_)
            attend_stage(nc, A, S, D_)
        if upto < 3:
            return
        S["meta"] = sb("meta", [P, META, 4], I32)
        S["more"] = sb("more", [P, 1], I32)
        S["b_gu"] = sb("b_gu", [P, 2 * FF // P, EXPERTS])
        S["pos"] = sb("pos", [P, TILES, TOP_E], I32)
        place_stage(nc, A, S, D_)
        experts_stage(nc, A, S, D_)
        combine_stage(nc, A, S, D_)


def constants():
    inv = np.concatenate([np.float32(THETA) ** (-np.arange(0, rd, 2, dtype=np.float32) / np.float32(rd))
                          for rd in (ROPE_D, IDX_ROPE_D)]).astype(np.float32)
    s, t = np.arange(P)[:, None], np.arange(P)[None, :]
    band = np.zeros((P, 3, POOL_GROUPS, P), np.float32)
    for g, w in enumerate(WINDOWS):
        inside = (t - s >= 0) & (t - s < w)
        band[:, 0, g] = inside / np.minimum(t + 1, w) - (s == t)
        band[:, 1, g] = inside / w - (s == t)
        band[:, 2, g] = (t - s + P < w) / w
    bit_value = np.array([[-1.0] + [2.0 ** (31 - i) for i in range(1, 32)]], np.float32)
    bit_next = np.array([[2 ** (30 - i) for i in range(31)] + [0]], np.int32)
    return {"inv_freq": inv, "band": band, "bit_value": bit_value, "bit_next": bit_next}


INPUTS = ("x", "positions", "ln_in_g", "ln_in_b", "w_in", "w_pool", "pool_scale", "w_out", "ln1_g", "ln1_b",
          "w_router", "b_router", "w_gate_up", "b_gate_up", "w_down", "b_down", "ln2_g", "ln2_b")


def kernel(**inputs):
    import concourse.bacc as bacc
    from concourse.bass_utils import run_bass_kernel_spmd

    nc = bacc.Bacc("TRN2", target_bir_lowering=False, num_devices=1)
    arrays = {name: np.ascontiguousarray(inputs[name]) for name in INPUTS}
    arrays.update(constants())
    args = {name: nc.dram_tensor(name, a.shape, mybir.dt.from_np(a.dtype), kind="ExternalInput").ap()
            for name, a in arrays.items()}
    args["out"] = nc.dram_tensor("out", (1, SEQ, D), F32, kind="ExternalOutput").ap()
    build(nc, args)
    return run_bass_kernel_spmd(nc, [arrays], core_ids=[0]).results[0]["out"]
```
